# Optimizing a Trainium2 kernel written in Bass

```python
import math
import jax
import jax.numpy as jnp
from jax import lax
import numpy as np

D_MODEL = 1024
BATCH = 1
SEQ = 256
DEPTH = 2
DEC_BATCH = 1
DEC_SEQ = 64
PAST_LEN = 256

CHUNK = 64
EPS = 1e-6
F32 = jnp.float32
D_RNN = 512
RNN_BLOCKS = 8
RNN_BLOCK = D_RNN // RNN_BLOCKS
CONV_W = 4
LRU_C = 8.0
D_POOL = 512
POOL_WINDOWS = (2, 4, 8, 16)
POOL_GROUPS = 4
POOL_GROUP = D_POOL // POOL_GROUPS
POOL_HIST = 15
N_HEADS = 8
HEAD_DIM = 64
ROT_DIM = HEAD_DIM // 4
ROPE_THETA = 500000.0
D_ATT = N_HEADS * 2 * HEAD_DIM
Q_BLOCK = 128
N_BRANCH = 3
IN_COLS = 2 * D_RNN + D_POOL + 3 * D_ATT + N_BRANCH * D_MODEL
PEER_HEADS = 8
D_KEY = 256
N_KEYS = 128
N_EXPERTS = N_KEYS * N_KEYS
PEER_TOPK = 16
PEER_BLOCK = 256

kernel_name = 'hybrid_rglru_pool_diffattn_peer_stream_step'

def rmsnorm(x, g):
    xf = x.astype(F32)
    y = xf * lax.rsqrt(jnp.mean(xf * xf, axis=-1, keepdims=True) + EPS)
    return (y * g.astype(F32)).astype(x.dtype)

def rotary(x, pos):
    half = ROT_DIM // 2
    inv = ROPE_THETA ** (-jnp.arange(half, dtype=F32) / half)
    ang = pos.astype(F32)[:, None] * inv[None, :]
    cos = jnp.cos(ang)[:, None, None, :]
    sin = jnp.sin(ang)[:, None, None, :]
    xr = x[..., :ROT_DIM].astype(F32)
    x1, x2 = xr[..., :half], xr[..., half:]
    rot = jnp.concatenate([x1 * cos - x2 * sin, x2 * cos + x1 * sin], axis=-1)
    return jnp.concatenate([rot.astype(x.dtype), x[..., ROT_DIM:]], axis=-1)

def causal_conv(x, hist, w, b):
    T = x.shape[1]
    xe = jnp.concatenate([hist, x], axis=1)
    y = b
    for j in range(CONV_W):
        y = y + xe[:, j:j + T] * w[j]
    return y, xe[:, -(CONV_W - 1):]

def rg_lru(x, h0, wa, ba, wx, bx, lru_L):
    B, T, _ = x.shape
    xb = x.reshape(B, T, RNN_BLOCKS, RNN_BLOCK)
    r = jax.nn.sigmoid((jnp.einsum('btgi,gij->btgj', xb, wa).reshape(B, T, D_RNN) + ba).astype(F32))
    i = jax.nn.sigmoid((jnp.einsum('btgi,gij->btgj', xb, wx).reshape(B, T, D_RNN) + bx).astype(F32))
    log_a = -LRU_C * r * jax.nn.softplus(-lru_L.astype(F32))
    a = jnp.exp(log_a)
    u = jnp.sqrt(-jnp.expm1(2.0 * log_a)) * i * x.astype(F32)
    u = u.at[:, 0].add(a[:, 0] * h0.astype(F32))

    def combine(p, q):
        a1, b1 = p
        a2, b2 = q
        return a1 * a2, a2 * b1 + b2

    _, h = lax.associative_scan(combine, (a, u), axis=1)
    return h.astype(x.dtype), h[:, -1].astype(x.dtype)

def pool_mixer(x, hist, pos0, w, scale):
    B, T, _ = x.shape
    xe_raw = jnp.concatenate([hist, x], axis=1)
    xe = xe_raw.astype(F32)
    cs = jnp.concatenate([jnp.zeros((B, 1, D_POOL), F32), jnp.cumsum(xe, axis=1)], axis=1)
    end = cs[:, POOL_HIST + 1:]
    pos = pos0 + jnp.arange(T)
    means = []
    for g, win in enumerate(POOL_WINDOWS):
        sl = slice(g * POOL_GROUP, (g + 1) * POOL_GROUP)
        start = cs[:, POOL_HIST + 1 - win:POOL_HIST + 1 - win + T, sl]
        cnt = jnp.minimum(pos + 1, win).astype(F32)[None, :, None]
        means.append((end[..., sl] - start) / cnt)
    mean = jnp.stack(means, axis=2)
    d = mean - x.reshape(B, T, POOL_GROUPS, POOL_GROUP).astype(F32)
    y = jnp.einsum('btgc,gcd->btgd', d, w.astype(F32)).reshape(B, T, D_POOL) * scale.astype(F32)
    return y.astype(x.dtype), xe_raw[:, -POOL_HIST:]

def diff_attn_block(q, k, v, q_pos, k_pos, lam):
    s = jnp.einsum('bqhmd,bkhmd->bhmqk', q, k).astype(F32) * (HEAD_DIM ** -0.5)
    mask = (k_pos[None, :] // CHUNK) <= (q_pos[:, None] // CHUNK)
    s = jnp.where(mask, s, -jnp.inf)
    p = jax.nn.softmax(s, axis=-1)
    p = p[:, :, 0] - lam * p[:, :, 1]
    return jnp.einsum('bhqk,bkhe->bqhe', p.astype(v.dtype), v)

def peer(h, wq, subkeys, u, v):
    B, T, D = h.shape
    n = B * T
    hf = h.reshape(n, D)
    q = (hf @ wq).reshape(n, PEER_HEADS, 2, D_KEY // 2)
    s = jnp.einsum('nhpd,pkd->nhpk', q, subkeys).astype(F32)
    top_s, top_i = lax.top_k(s, PEER_TOPK)
    cand = (top_s[:, :, 0, :, None] + top_s[:, :, 1, None, :]).reshape(n, PEER_HEADS, PEER_TOPK * PEER_TOPK)
    best_s, best_c = lax.top_k(cand, PEER_TOPK)
    i1 = jnp.take_along_axis(top_i[:, :, 0], best_c // PEER_TOPK, axis=-1)
    i2 = jnp.take_along_axis(top_i[:, :, 1], best_c % PEER_TOPK, axis=-1)
    idx = i1 * N_KEYS + i2
    gate = jax.nn.softmax(best_s, axis=-1).astype(h.dtype)
    nb = -(-n // PEER_BLOCK)
    pad = nb * PEER_BLOCK - n
    hp = jnp.pad(hf, ((0, pad), (0, 0))).reshape(nb, PEER_BLOCK, D)
    ip = jnp.pad(idx, ((0, pad), (0, 0), (0, 0))).reshape(nb, PEER_BLOCK, PEER_HEADS, PEER_TOPK)
    gp = jnp.pad(gate, ((0, pad), (0, 0), (0, 0))).reshape(nb, PEER_BLOCK, PEER_HEADS, PEER_TOPK)

    def expert_block(args):
        xb, ib, gb = args
        act = jax.nn.gelu(jnp.einsum('nd,nhkd->nhk', xb, u[ib]), approximate=False)
        return jnp.einsum('nhk,nhkd->nd', gb * act, v[ib])

    out = lax.map(expert_block, (hp, ip, gp)).reshape(nb * PEER_BLOCK, D)[:n]
    return out.reshape(B, T, D)

def layer(x, pos0, conv_hist, lru_h0, pool_hist, k_past, v_past, lam_init,
          norm1_g, w_in, conv_w, conv_b, lru_wa, lru_ba, lru_wx, lru_bx, lru_L,
          pool_w, pool_scale, lam_q1, lam_k1, lam_q2, lam_k2, subln_g,
          proj_a, proj_b, proj_c, w_out, norm2_g, peer_wq, peer_subkeys, peer_u, peer_v):
    B, T, _ = x.shape
    h = rmsnorm(x, norm1_g)
    z = h @ w_in
    cuts = [D_RNN, 2 * D_RNN, 2 * D_RNN + D_POOL, 2 * D_RNN + D_POOL + D_ATT,
            2 * D_RNN + D_POOL + 2 * D_ATT, 2 * D_RNN + D_POOL + 3 * D_ATT]
    xa, ga, xq, qf, kf, vf, gates = jnp.split(z, cuts, axis=-1)
    xc, conv_state = causal_conv(xa, conv_hist, conv_w, conv_b)
    ha, lru_state = rg_lru(xc, lru_h0, lru_wa, lru_ba, lru_wx, lru_bx, lru_L)
    ya = ha * jax.nn.gelu(ga, approximate=False)
    yb, pool_state = pool_mixer(xq, pool_hist, pos0, pool_w, pool_scale)
    pos = pos0 + jnp.arange(T)
    q = rotary(qf.reshape(B, T, N_HEADS, 2, HEAD_DIM), pos)
    k = rotary(kf.reshape(B, T, N_HEADS, 2, HEAD_DIM), pos)
    v = vf.reshape(B, T, N_HEADS, 2 * HEAD_DIM)
    lam = (jnp.exp(jnp.sum(lam_q1.astype(F32) * lam_k1.astype(F32)))
           - jnp.exp(jnp.sum(lam_q2.astype(F32) * lam_k2.astype(F32))) + lam_init)
    if k_past is None:
        outs = []
        for qb in range(T // Q_BLOCK):
            lo, hi = qb * Q_BLOCK, (qb + 1) * Q_BLOCK
            outs.append(diff_attn_block(q[:, lo:hi], k[:, :hi], v[:, :hi], pos[lo:hi], pos[:hi], lam))
        o = jnp.concatenate(outs, axis=1)
    else:
        k_all = jnp.concatenate([k_past, k], axis=1)
        v_all = jnp.concatenate([v_past, v], axis=1)
        o = diff_attn_block(q, k_all, v_all, pos, jnp.arange(k_all.shape[1]), lam)
    o = rmsnorm(o, subln_g) * (1.0 - lam_init)
    yc = o.reshape(B, T, D_ATT)
    g = jax.nn.sigmoid(gates.astype(F32)).astype(x.dtype).reshape(B, T, N_BRANCH, D_MODEL)
    m = g[:, :, 0] * (ya @ proj_a) + g[:, :, 1] * (yb @ proj_b) + g[:, :, 2] * (yc @ proj_c)
    x = x + m @ w_out
    x = x + peer(rmsnorm(x, norm2_g), peer_wq, peer_subkeys, peer_u, peer_v)
    return x, k, v, conv_state, lru_state, pool_state

def setup_inputs(seed: int = 0) -> dict:
    key = jax.random.key(seed)
    ks = iter(jax.random.split(key, 40))
    nrm = lambda shape, s: jax.random.normal(next(ks), shape, F32) * s
    a0 = jax.random.uniform(next(ks), (DEPTH, D_RNN), F32, minval=0.9, maxval=0.999)
    sg = a0 ** (1.0 / LRU_C)
    return {
        'x_prompt': nrm((BATCH, SEQ, D_MODEL), 1.0),
        'x_sample': nrm((DEC_BATCH, DEC_SEQ, D_MODEL), 1.0),
        'cache_k': nrm((DEPTH, DEC_BATCH, PAST_LEN, N_HEADS, 2, HEAD_DIM), 1.0),
        'cache_v': nrm((DEPTH, DEC_BATCH, PAST_LEN, N_HEADS, 2 * HEAD_DIM), 1.0),
        'state_conv': nrm((DEPTH, DEC_BATCH, CONV_W - 1, D_RNN), 1.0),
        'state_lru': nrm((DEPTH, DEC_BATCH, D_RNN), 0.5),
        'state_pool': nrm((DEPTH, DEC_BATCH, POOL_HIST, D_POOL), 1.0),
        'norm1_g': 1.0 + nrm((DEPTH, D_MODEL), 0.02),
        'w_in': nrm((DEPTH, D_MODEL, IN_COLS), D_MODEL ** -0.5),
        'conv_w': nrm((DEPTH, CONV_W, D_RNN), CONV_W ** -0.5),
        'conv_b': nrm((DEPTH, D_RNN), 0.01),
        'lru_wa': nrm((DEPTH, RNN_BLOCKS, RNN_BLOCK, RNN_BLOCK), RNN_BLOCK ** -0.5),
        'lru_ba': nrm((DEPTH, D_RNN), 0.01),
        'lru_wx': nrm((DEPTH, RNN_BLOCKS, RNN_BLOCK, RNN_BLOCK), RNN_BLOCK ** -0.5),
        'lru_bx': nrm((DEPTH, D_RNN), 0.01),
        'lru_L': jnp.log(sg) - jnp.log1p(-sg),
        'pool_w': nrm((DEPTH, POOL_GROUPS, POOL_GROUP, POOL_GROUP), POOL_GROUP ** -0.5),
        'pool_scale': 1.0 + nrm((DEPTH, D_POOL), 0.02),
        'lam_q1': nrm((DEPTH, HEAD_DIM), 0.1),
        'lam_k1': nrm((DEPTH, HEAD_DIM), 0.1),
        'lam_q2': nrm((DEPTH, HEAD_DIM), 0.1),
        'lam_k2': nrm((DEPTH, HEAD_DIM), 0.1),
        'subln_g': 1.0 + nrm((DEPTH, 2 * HEAD_DIM), 0.02),
        'proj_a': nrm((DEPTH, D_RNN, D_MODEL), D_RNN ** -0.5),
        'proj_b': nrm((DEPTH, D_POOL, D_MODEL), D_POOL ** -0.5),
        'proj_c': nrm((DEPTH, D_ATT, D_MODEL), D_ATT ** -0.5),
        'w_out': nrm((DEPTH, D_MODEL, D_MODEL), D_MODEL ** -0.5),
        'norm2_g': 1.0 + nrm((DEPTH, D_MODEL), 0.02),
        'peer_wq': nrm((DEPTH, D_MODEL, PEER_HEADS * D_KEY), D_MODEL ** -0.5),
        'peer_subkeys': nrm((DEPTH, 2, N_KEYS, D_KEY // 2), (D_KEY // 2) ** -0.5),
        'peer_u': nrm((DEPTH, N_EXPERTS, D_MODEL), D_MODEL ** -0.5),
        'peer_v': nrm((DEPTH, N_EXPERTS, D_MODEL), PEER_HEADS ** -0.5),
        'final_g': 1.0 + nrm((D_MODEL,), 0.02),
    }

def reference(x_prompt, x_sample, cache_k, cache_v, state_conv, state_lru, state_pool,
              norm1_g, w_in, conv_w, conv_b, lru_wa, lru_ba, lru_wx, lru_bx, lru_L,
              pool_w, pool_scale, lam_q1, lam_k1, lam_q2, lam_k2, subln_g,
              proj_a, proj_b, proj_c, w_out, norm2_g, peer_wq, peer_subkeys, peer_u, peer_v,
              final_g):
    Bp, Tp, _ = x_prompt.shape
    dt = x_prompt.dtype
    past = cache_k.shape[2]
    keep = min(Tp, past)
    xp, xs = x_prompt, x_sample
    kp, vp, cp, lp, pp = [], [], [], [], []
    ks_, vs_, cs_, ls_, ps_ = [], [], [], [], []
    for l in range(DEPTH):
        lam_init = 0.8 - 0.6 * math.exp(-0.3 * l)
        w = (norm1_g[l], w_in[l], conv_w[l], conv_b[l], lru_wa[l], lru_ba[l], lru_wx[l], lru_bx[l],
             lru_L[l], pool_w[l], pool_scale[l], lam_q1[l], lam_k1[l], lam_q2[l], lam_k2[l],
             subln_g[l], proj_a[l], proj_b[l], proj_c[l], w_out[l], norm2_g[l], peer_wq[l],
             peer_subkeys[l], peer_u[l], peer_v[l])
        xp, k1, v1, c1, h1, p1 = layer(
            xp, 0, jnp.zeros((Bp, CONV_W - 1, D_RNN), dt), jnp.zeros((Bp, D_RNN), dt),
            jnp.zeros((Bp, POOL_HIST, D_POOL), dt), None, None, lam_init, *w)
        kp.append(k1[:, Tp - keep:])
        vp.append(v1[:, Tp - keep:])
        cp.append(c1)
        lp.append(h1)
        pp.append(p1)
        xs, k2, v2, c2, h2, p2 = layer(
            xs, past, state_conv[l], state_lru[l], state_pool[l], cache_k[l], cache_v[l], lam_init, *w)
        ks_.append(k2)
        vs_.append(v2)
        cs_.append(c2)
        ls_.append(h2)
        ps_.append(p2)
    y_prompt = rmsnorm(xp, final_g)
    y_sample = rmsnorm(xs, final_g)
    return (y_prompt, y_sample,
            jnp.stack(kp), jnp.stack(vp), jnp.stack(cp), jnp.stack(lp), jnp.stack(pp),
            jnp.stack(ks_), jnp.stack(vs_), jnp.stack(cs_), jnp.stack(ls_), jnp.stack(ps_))


_drawn_inputs = setup_inputs


def setup_inputs(seed=0):
    import zlib

    import numpy as np

    out = dict(_drawn_inputs(seed))
    spreads = {}
    factors = {'lru_ba': 24.534, 'lru_bx': 8.0, 'lam_k1': 4.035, 'final_g': 7.534}
    for name, (base, spread) in spreads.items():
        noise = np.random.default_rng([zlib.crc32(name.encode()), seed]).standard_normal(out[name].shape)
        drawn = base * np.exp(spread * noise) if base else spread * noise
        out[name] = jnp.asarray(drawn.astype(out[name].dtype))
    for name, factor in factors.items():
        out[name] = (out[name] * factor).astype(out[name].dtype)
    return out
```

```python
from contextlib import ExitStack

import numpy as np

import concourse.bass as bass
from concourse import mybir

F32 = mybir.dt.float32
U32 = mybir.dt.uint32
ALU = mybir.AluOpType
ACT = mybir.ActivationFunctionType
AX_X = mybir.AxisListType.X

P = 128
DEPTH, D_MODEL, SEQ, DEC_SEQ, PAST = 2, 1024, 256, 64, 256
TOK = SEQ + DEC_SEQ
TILES = 3
TOKD = TILES * P
KC = D_MODEL // P
D_RNN = D_POOL = 512
RC = D_RNN // P
CONV_W, POOL_HIST, CHUNK = 4, 15, 64
HEADS, HD = 8, 64
HW = 2 * HD
ROT = HD // 8
N_BRANCH = 3
COL_Q = 2 * D_RNN + D_POOL
COL_G = COL_Q + 3 * HEADS * HW
PH, NK, TOPK = 8, 128, 16
N_EXPERTS = NK * NK
EPS = 1e-6
LRU_C = 8.0
FAR = -1e30
LOW = -3e38
SCALE = HD ** -0.5

CONV_HIST = CONV_W - 1
XA_S = CONV_HIST + SEQ
XA_W = XA_S + CONV_HIST + DEC_SEQ
XC_W = XA_W - CONV_HIST
XQ_S = POOL_HIST + SEQ
XQ_W = XQ_S + POOL_HIST + DEC_SEQ

ROW = dict(conv_state=0, pool_state=3, lru_state=18, conv_w=19, conv_b=23, lru_ba=24, lru_bx=25,
           lru_L=26, pool_scale=27)
NROW = 28
ST_CP, ST_PP, ST_CS, ST_PS, ST_LP, ST_LS = 0, 3, 18, 21, 36, 37

UNIT = 256
SLOTS = 5
HB = D_RNN // UNIT
GB = D_MODEL // UNIT
SLOT_USES = [2 + GB + 1 + 2] + [1 + GB + 1 + 2] * 3 + [1 + GB]

BATCH = 8
TILE_B = [P // BATCH, P // BATCH, P // BATCH // 2]
BATCHES = sum(TILE_B)


class Signal:

    def __init__(self, sem, per_layer, unit=1, start=0):
        self.sem, self.per_layer, self.unit, self.start = sem, per_layer, unit, start

    def at(self, l, n):
        return self.sem, (l * self.per_layer + n) * self.unit + self.start


def build(nc, x_prompt, x_sample, cache_k, cache_v, state_conv, state_lru, state_pool,
          norm1_g, w_in, conv_w, conv_b, lru_wa, lru_ba, lru_wx, lru_bx, lru_L,
          pool_w, pool_scale, lam_q1, lam_k1, lam_q2, lam_k2, subln_g,
          proj_a, proj_b, proj_c, w_out, norm2_g, peer_wq, peer_subkeys, peer_u, peer_v,
          final_g, rot_table, pool_inv, layer_consts,
          y_prompt, y_sample, k_prompt, v_prompt, conv_prompt, lru_prompt, pool_prompt,
          k_sample, v_sample, conv_sample, lru_sample, pool_sample):
    ctx = ExitStack()
    with ctx:
        def sb(name, shape, dt=F32):
            return ctx.enter_context(nc.sbuf_tensor(name, shape, dt))

        started = []

        def signal(name, per_layer, unit=1, start=0):
            s = Signal(ctx.enter_context(nc.semaphore(name)), per_layer, unit, start)
            if start:
                started.append(s)
            return s

        def landing(name, per_layer):
            return signal(name, per_layer, 16)

        def parts(name, size):
            t = sb(name, [P, size])
            used = [0]

            def cut(*shape, at=None):
                n = int(np.prod(shape))
                a = used[0] if at is None else at
                assert a + n <= size, (name, a, n)
                used[0] = a + n
                v = t[:, a:a + n]
                names = "abc"[:len(shape)]
                if len(shape) > 1:
                    v = v.rearrange(f"p ({' '.join(names)}) -> p {' '.join(names)}",
                                    **{names[i]: shape[i] for i in range(len(shape))})
                return v
            return cut

        X = sb("X", [P, TILES, D_MODEL])
        HT = sb("HT", [P, KC, TOKD])
        G = sb("G", [P, D_MODEL])
        cut = parts("YT_HN", (4 + 4 + 8) * TOK)
        YT = cut(16, TOK)
        HN = cut(TILES, D_MODEL, at=0)
        DG = cut(BATCH, P)
        STG = cut(2, NK)
        STG2 = cut(2, NK)
        CAND = cut(TOPK, TOPK)
        CAND2 = cut(TOPK, TOPK)
        W = sb("W", [P, SLOTS, KC, UNIT])
        cut = parts("WQ_SALL", 2 * KC * 3 * HW)
        WQKV = cut(2, KC * 3 * HW)
        WQKV = [WQKV[:, i, :].rearrange("p (c n) -> p c n", c=KC) for i in range(2)]
        SALL = cut(TILES, 2 * PH, NK, at=0)
        cut = parts("MIX_RINGS", 2 * BATCH * D_MODEL)
        RING_U = cut(BATCH, D_MODEL)
        RING_V = cut(BATCH, D_MODEL)
        XA = cut(RC, XA_W, at=0)
        XC = cut(RC, XC_W)
        RG = cut(RC, XC_W)
        IG = cut(RC, XC_W)
        DEC = cut(RC, XC_W)
        XQ = cut(RC, XQ_W)
        S1 = cut(RC, XQ_W)
        S2 = cut(RC, XQ_W)
        OALL = cut(TILES, HEADS, HW)
        ZH = cut(2, TILES * 3 * HW)
        ZH = [ZH[:, i, :].rearrange("p (t n) -> p t n", t=TILES) for i in range(2)]
        SUMS = [(S1, S2)[c % 2][:, c, :] for c in range(RC)]
        POOL_PARTS = ((POOL_HIST, SEQ, 0), (XQ_S + POOL_HIST, DEC_SEQ, SEQ))
        MT = cut(KC, TOKD, at=0)
        SQ = cut(TILES, HEADS, HW)
        SG = cut(N_BRANCH, TOK)
        MTMP = cut(TOK)
        QS = cut(2, TOKD, at=0)
        QT = cut(2, TOKD, at=0)
        KT = cut(2 * PAST + P)
        PR = [cut(2, P), cut(2, 2 * P), cut(2, PAST + DEC_SEQ)]
        PC = [cut(P), cut(2 * P), cut(3 * P)]
        PTA = cut(3 * P)
        PTB = cut(3 * P)
        rows = cut(D_RNN, at=10672)
        SKR = cut(2, NK)
        LAMV = cut(4, HD)
        POOLW = cut(RC, P)

        PT = sb("PT", [P, RC, NROW])
        nsp = sb("nsp", [P, RC])
        spt = sb("spt", [P, 3, RC])
        SKT = sb("SKT", [P, 2, NK])
        BDA = sb("BDA", [P, RC, P])
        BDX = sb("BDX", [P, RC, P])
        SO = sb("SO", [P, RC, P])
        SOT = sb("SOT", [P, D_RNN])
        LD = sb("LD", [P, 2])
        LE = sb("LE", [P, 2])
        neg_lam = sb("neg_lam", [P, 1])
        LCON = sb("LCON", [P, 3])
        SUBG = sb("SUBG", [P, HW])
        ident = sb("ident", [P, P])
        twins = sb("twins", [P, P])
        mask_q = sb("mask_q", [P, P])
        mask_k = sb("mask_k", [P, 2, P])
        eps_c = sb("eps_c", [P, 1])
        iota16 = sb("iota16", [P, TOPK])
        ROTT = sb("ROTT", [P, TILES, 2, ROT])
        PINV = sb("PINV", [P, 4, TOK])
        ss = sb("ss", [P, TILES])
        sd = sb("sd", [P, TILES])
        rstd = sb("rstd", [P, TILES])
        sso = sb("sso", [P, TILES, HEADS])
        rso = sb("rso", [P, TILES, HEADS])

        CKV = sb("CKV", [P, 2, 2, 2, HW])
        CK = [CKV[:, i, 0] for i in range(2)]
        CV = [CKV[:, i, 1] for i in range(2)]
        HOT = sb("HOT", [P, 2, TOPK * TOPK])
        rot_a = sb("rot_a", [P, 4, TILES, 4, ROT])
        mxs = sb("mxs", [P, TILES, 2])
        nb = sb("nb", [P, TILES, 2])
        sme = sb("sme", [P, TILES, 2])
        rec = sb("rec", [P, TILES, 2])
        MX = sb("MX", [P, 2, TOPK])
        IX = sb("IX", [P, 2, TOPK], U32)
        IXF = sb("IXF", [P, 2, TOPK])
        BS = sb("BS", [P, TOPK])
        BC = sb("BC", [P, TOPK], U32)
        CI = sb("CI", [P, 2, TOPK], U32)
        CIF = sb("CIF", [P, 2, TOPK])
        I12 = sb("I12", [P, 2, TOPK])
        IDF = sb("IDF", [P, TOPK])
        IDX = sb("IDX", [P, TOPK], U32)
        STI = sb("STI", [P, 2, BATCH], U32)
        BSM = sb("BSM", [P, TOPK])
        GEX = sb("GEX", [P, TOPK])
        GSM = sb("GSM", [P, 1])
        GRC = sb("GRC", [P, 1])
        GATE = sb("GATE", [P, TOPK])
        AV = sb("AV", [P, BATCH])
        GV = sb("GV", [P, BATCH])
        WV = sb("WV", [P, BATCH])

        ps = ctx.enter_context(nc.psum_tensor("ps", [P, 8 * 512], F32))

        def bank(i, a=0, b=512):
            return ps[:, i * 512 + a:i * 512 + b]

        setup = signal("setup", 0)
        loaded_x = landing("loaded_x", 0)
        gain_in = landing("gain_in", 2)
        gain_used = signal("gain_used", 1)
        w_in_slot = [landing(f"w_in_slot{i}", SLOT_USES[i]) for i in range(SLOTS)]
        w_used = [signal(f"w_used{i}", SLOT_USES[i], start=1) for i in range(SLOTS)]
        qkv_in = [landing(f"qkv_in{i}", 3 * HEADS // 2) for i in range(2)]
        qkv_used = [signal(f"qkv_used{i}", HEADS // 2, start=1) for i in range(2)]
        cache_in = [landing(f"cache_in{i}", 2 * HEADS // 2) for i in range(2)]
        layer_done = signal("layer_done", 4, start=1)
        par_ps = signal("par_ps", 2)
        par_sb = signal("par_sb", 2)
        lam_dot = signal("lam_dot", 1)
        lam_exp = signal("lam_exp", 1)
        sp_in = signal("sp_in", 1)
        sp_ln = signal("sp_ln", 1)
        sp_out = signal("sp_out", 1)
        sq_done = signal("sq_done", 2)
        hn_ready = signal("hn_ready", 2)
        nt_ps = signal("nt_ps", 2 * KC)
        nt_ev = signal("nt_ev", 2 * KC)
        ff_ps = signal("ff_ps", 12)
        ff_ev = signal("ff_ev", 12)
        xc_ready = signal("xc_ready", 1)
        bd_ps = signal("bd_ps", 2 * RC)
        sig_ev = signal("sig_ev", 2 * RC)
        decay = signal("decay", 1)
        oma = signal("oma", 1)
        root = signal("root", 1)
        ya_ready = signal("ya_ready", 1)
        d_ready = signal("d_ready", 1)
        pl_ps = signal("pl_ps", RC)
        pl_ev = signal("pl_ev", RC)
        so_ready = signal("so_ready", 1)
        so_ps = signal("so_ps", 1)
        so_sb = signal("so_sb", 1)
        so_out = landing("so_out", 6)
        z_ps = signal("z_ps", TILES * HEADS)
        z_ev = signal("z_ev", TILES * HEADS)
        rot_mul = signal("rot_mul", 4 * HEADS)
        rot_done = signal("rot_done", 2 * HEADS, start=1)
        kv_out = [landing(f"kv_out{i}", 4 * HEADS // 2) for i in range(2)]
        kv_stored = signal("kv_stored", HEADS, start=1)
        qt_ps = signal("qt_ps", HEADS)
        qt_ev = signal("qt_ev", 2 * HEADS)
        kt_ps = signal("kt_ps", HEADS)
        kt_ev = signal("kt_ev", HEADS)
        s_ps = signal("s_ps", TILES * HEADS)
        nb_ready = signal("nb_ready", TILES * HEADS)
        ex_done = signal("ex_done", 2 * TILES * HEADS, start=1)
        p_ready = signal("p_ready", TILES * HEADS)
        pta_ps = signal("pta_ps", HEADS)
        ptb_ps = signal("ptb_ps", HEADS)
        pta_ev = signal("pta_ev", HEADS, start=1)
        ptb_ev = signal("ptb_ev", HEADS, start=1)
        att_done = signal("att_done", HEADS, start=1)
        cache_free = signal("cache_free", HEADS, start=2)
        o_ev = signal("o_ev", HEADS, start=1)
        sso_ready = signal("sso_ready", 1)
        sso_root = signal("sso_root", 1)
        on_ready = signal("on_ready", 1)
        yt_ps = signal("yt_ps", HEADS)
        yt_ev = signal("yt_ev", HEADS)
        projab_in = landing("projab_in", GB)
        gate_ps = signal("gate_ps", N_BRANCH * KC)
        sg_ev = signal("sg_ev", N_BRANCH * KC, start=1)
        proj_ps = signal("proj_ps", KC)
        m_ev = signal("m_ev", KC, start=1)
        mt_ready = signal("mt_ready", 1)
        xo_ps = signal("xo_ps", GB * TILES)
        xo_ev = signal("xo_ev", GB * TILES)
        pq_ps = signal("pq_ps", 2 * PH)
        pq_ev = signal("pq_ev", 2 * PH)
        sc_ps = signal("sc_ps", 2 * PH)
        sc_ev = signal("sc_ev", 2 * PH, start=1)
        best_ready = signal("best_ready", TILES * PH)
        gex_ready = signal("gex_ready", TILES * PH)
        idx_staged = signal("idx_staged", BATCHES)
        u_in = [landing(f"u_in{i}", BATCHES) for i in range(BATCH)]
        v_in = [landing(f"v_in{i}", BATCHES) for i in range(BATCH)]
        u_free = signal("u_free", BATCHES * BATCH, start=BATCH)
        v_free = signal("v_free", BATCHES * BATCH, start=BATCH)
        av_ready = signal("av_ready", BATCHES)
        gv_ready = signal("gv_ready", BATCHES)
        wv_ready = signal("wv_ready", BATCHES)
        dg_ready = signal("dg_ready", BATCHES * BATCH)
        acc_clear = signal("acc_clear", TILES)
        y_ready = signal("y_ready", 0)
        stored = landing("stored", 0)

        def bcast(row):
            return row.partition_broadcast(P)

        def small_loads(l):
            def row(name, n=1):
                return rows[ROW[name]:ROW[name] + n, :]

            def diag(t, half):
                a = half * HD
                return t[a:a + HD, :, a:a + HD]

            def blocks(w, half):
                return w[l].rearrange("(c two) i j -> two i c j", two=2)[half]

            return [
                (row("conv_state", CONV_HIST), state_conv[l, 0]),
                (row("pool_state", POOL_HIST), state_pool[l, 0]),
                (row("lru_state"), state_lru[l]),
                (row("conv_w", CONV_W), conv_w[l]),
                (row("conv_b"), conv_b[bass.ds(l, 1)]),
                (row("lru_ba"), lru_ba[bass.ds(l, 1)]),
                (row("lru_bx"), lru_bx[bass.ds(l, 1)]),
                (row("lru_L"), lru_L[bass.ds(l, 1)]),
                (row("pool_scale"), pool_scale[bass.ds(l, 1)]),
                (SKR[:, :, :], peer_subkeys[l].rearrange("a k d -> k a d")),
                (POOLW[:, :, :], pool_w[l].rearrange("g c d -> c g d")),
                (diag(BDA, 0), blocks(lru_wa, 0)),
                (diag(BDA, 1), blocks(lru_wa, 1)),
                (diag(BDX, 0), blocks(lru_wx, 0)),
                (diag(BDX, 1), blocks(lru_wx, 1)),
                (LAMV[:, 0, :], bcast(lam_q1[l])),
                (LAMV[:, 1, :], bcast(lam_k1[l])),
                (LAMV[:, 2, :], bcast(lam_q2[l])),
                (LAMV[:, 3, :], bcast(lam_k2[l])),
                (LCON[:, :], bcast(layer_consts[l])),
                (SUBG[:, :], bcast(subln_g[l])),
            ]

        NSMALL = 21
        small_in = landing("small_in", NSMALL)
        block = ctx.enter_context(nc.Block())

        @block.sync
        def _(sp):
            sp.dma_start(X[:, 0:2, :], x_prompt[0].rearrange("(t p) d -> p t d", p=P))\
                .then_inc(loaded_x.sem, 16)
            sp.dma_start(X[0:CHUNK, 2, :], x_sample[0]).then_inc(loaded_x.sem, 16)
            sp.dma_start(X[CHUNK:P, 2, :], x_sample[0]).then_inc(loaded_x.sem, 16)
            sp.dma_start(ROTT[:, :, :, :], rot_table.rearrange("t p a r -> p t a r"))\
                .then_inc(loaded_x.sem, 16)
            sp.dma_start(PINV[:, :, :], pool_inv.partition_broadcast(P)).then_inc(loaded_x.sem, 16)
            sp.wait_ge(setup.sem, 10)

            def unit(l, slot, n, srcs):
                sp.wait_ge(*w_used[slot].at(l, n))
                at = 0
                for k, src in enumerate(srcs):
                    c = src.shape[0] // P
                    i = sp.dma_start(W[:, slot, at:at + c, :], src.rearrange("(c p) n -> p c n", p=P))
                    at += c
                    i.then_inc(w_in_slot[slot].sem, 16)

            with sp.Fori(0, DEPTH) as l:
                def ff_unit(u):
                    kind, j = u % 3, u // 3
                    unit(l, u % SLOTS, u // SLOTS,
                         [w_in[l, :, kind * D_RNN + j * UNIT:kind * D_RNN + (j + 1) * UNIT]])

                for u in range(SLOTS):
                    ff_unit(u)
                sp.wait_ge(*layer_done.at(l, 0))
                sp.dma_start(G[:, :], bcast(norm1_g[l])).then_inc(gain_in.sem, 16)
                loads = small_loads(l)
                assert len(loads) == NSMALL
                for dst, src in loads:
                    sp.dma_start(dst, src).then_inc(small_in.sem, 16)
                for u in range(SLOTS, 3 * HB):
                    ff_unit(u)

                with sp.Fori(0, HEADS // 2) as g:
                    for par in range(2):
                        h = g * 2 + par
                        sp.wait_ge(*qkv_used[par].at(l, g))
                        for part in range(3):
                            col = COL_Q + part * HEADS * HW + h * HW
                            sp.dma_start(
                                WQKV[par][:, :, part * HW:(part + 1) * HW],
                                w_in[l, :, bass.ds(col, HW)].rearrange("(c p) n -> p c n", p=P))\
                                .then_inc(qkv_in[par].sem, 16)
                        sp.wait_ge(*cache_free.at(l, h - 1))
                        sp.dma_start(CK[par], cache_k[l, 0, :, h].rearrange("(t p) m d -> p t (m d)", p=P))\
                            .then_inc(cache_in[par].sem, 16)
                        sp.dma_start(CV[par], cache_v[l, 0, :, h].rearrange("(t p) e -> p t e", p=P))\
                            .then_inc(cache_in[par].sem, 16)

                sp.wait_ge(*gain_used.at(l, 1))
                sp.dma_start(G[:, :], bcast(norm2_g[l])).then_inc(gain_in.sem, 16)
                with sp.Fori(0, GB) as i:
                    for b in range(N_BRANCH):
                        sp.wait_ge(*w_used[b].at(l, i + (2 if b == 0 else 1)))
                        sp.dma_start(W[:, b, :, :],
                                     w_in[l, :, bass.ds(COL_G + b * D_MODEL + i * UNIT, UNIT)]
                                     .rearrange("(c p) n -> p c n", p=P)).then_inc(w_in_slot[b].sem, 16)
                    sp.wait_ge(*w_used[3].at(l, i + 1))
                    sp.dma_start(W[:, 3, 0:RC, :], proj_a[l, :, bass.ds(i * UNIT, UNIT)]
                                 .rearrange("(c p) n -> p c n", p=P)).then_inc(projab_in.sem, 16)
                    sp.dma_start(W[:, 3, RC:2 * RC, :], proj_b[l, :, bass.ds(i * UNIT, UNIT)]
                                 .rearrange("(c p) n -> p c n", p=P)).then_inc(w_in_slot[3].sem, 16)
                    sp.wait_ge(*w_used[4].at(l, i + 1))
                    sp.dma_start(W[:, 4, :, :], proj_c[l, :, bass.ds(i * UNIT, UNIT)]
                                 .rearrange("(c p) n -> p c n", p=P)).then_inc(w_in_slot[4].sem, 16)
                for u in range(GB):
                    unit(l, u, GB + (2 if u == 0 else 1), [w_out[l, :, u * UNIT:(u + 1) * UNIT]])
                with sp.Fori(0, 2) as i:
                    for j in range(4):
                        sp.wait_ge(*w_used[j].at(l, i + GB + (3 if j == 0 else 2)))
                        sp.dma_start(W[:, j, :, :], peer_wq[l, :, bass.ds(i * 4 * UNIT + j * UNIT, UNIT)]
                                     .rearrange("(c p) n -> p c n", p=P)).then_inc(w_in_slot[j].sem, 16)
            sp.wait_ge(*layer_done.at(DEPTH, 0))
            sp.dma_start(G[:, :], bcast(final_g)).then_inc(gain_in.sem, 16)
            sp.wait_ge(y_ready.sem, 1)
            sp.dma_start(y_prompt[0].rearrange("(t p) d -> p t d", p=P), HN[:, 0:2, :]).then_inc(stored.sem, 16)
            sp.dma_start(y_sample[0], HN[0:DEC_SEQ, 2, :]).then_inc(stored.sem, 16)
            sp.wait_ge(stored.sem, 32)

        @block.gpsimd
        def _(pool):
            for s in started:
                pool.sem_inc(s.sem, s.start)
            pool.memset(ident[:, :], 0.0).then_inc(setup.sem, 1)
            pool.memset(twins[:, :], 0.0).then_inc(setup.sem, 1)
            pool.memset(rows[:, :], 0.0).then_inc(setup.sem, 1)
            pool.memset(BDA[:, :, :], 0.0).then_inc(setup.sem, 1)
            pool.memset(BDX[:, :, :], 0.0).then_inc(setup.sem, 1)
            pool.memset(SO[:, :, :], 0.0).then_inc(setup.sem, 1)
            pool.memset(mask_q[:, :], 0.0).then_inc(setup.sem, 1)
            pool.memset(mask_k[:, :, :], 0.0).then_inc(setup.sem, 1)
            pool.memset(eps_c[:, :], EPS).then_inc(setup.sem, 1)
            pool.memset(iota16[:, :], 0.0).then_inc(setup.sem, 1)
            pool.wait_ge(setup.sem, 10)
            pool.affine_select(out=ident[:, :], in_=ident[:, :], compare_op=ALU.not_equal, fill=1.0,
                               base=0, pattern=[[-1, P]], channel_multiplier=1).then_inc(setup.sem, 1)
            pool.memset(mask_q[0:1, 0:CHUNK], 1.0).then_inc(setup.sem, 1)
            pool.memset(mask_k[:, 1, CHUNK:P], FAR).then_inc(setup.sem, 1)
            pool.iota(iota16[:, :], [[1, TOPK]], base=0, channel_multiplier=0,
                      allow_small_or_imprecise_dtypes=True).then_inc(setup.sem, 1)
            for n, base in enumerate((0, CHUNK, -CHUNK)):
                pool.affine_select(out=twins[:, :], in_=twins[:, :], compare_op=ALU.not_equal, fill=1.0,
                                   base=base, pattern=[[-1, P]], channel_multiplier=1).then_inc(setup.sem, 1)
                pool.wait_ge(setup.sem, 15 + n)
            pool.wait_ge(loaded_x.sem, 5 * 16)

            def rotary(l, h_before, par):
                h = h_before * 2 + par
                z = ZH[par][:, :, 0:2 * HW].rearrange("p t (m d) -> p t m d", m=4)
                x1, x2 = z[:, :, :, 0:ROT], z[:, :, :, ROT:2 * ROT]
                cos = ROTT[:, :, 0, :].unsqueeze(2).to_broadcast([P, TILES, 4, ROT])
                sin = ROTT[:, :, 1, :].unsqueeze(2).to_broadcast([P, TILES, 4, ROT])
                pool.wait_ge(*z_ev.at(l, h * TILES + TILES))
                pool.wait_ge(*rot_done.at(l, h * 2))
                for n, (a, b) in enumerate(((x1, cos), (x2, sin), (x2, cos), (x1, sin))):
                    pool.tensor_tensor(rot_a[:, n], a, b, ALU.mult).then_inc(rot_mul.sem, 1)
                pool.wait_ge(*rot_mul.at(l, h * 4 + 4))
                pool.tensor_tensor(x1, rot_a[:, 0], rot_a[:, 1], ALU.subtract).then_inc(rot_done.sem, 1)
                pool.tensor_tensor(x2, rot_a[:, 2], rot_a[:, 3], ALU.add).then_inc(rot_done.sem, 1)
                pool.wait_ge(*rot_done.at(l, h * 2 + 2))
                kcol, vcol = slice(HW, 2 * HW), slice(2 * HW, 3 * HW)
                pool.dma_start(k_prompt[l, 0, :, h].rearrange("(t p) m d -> p t (m d)", p=P),
                               ZH[par][:, 0:2, kcol]).then_inc(kv_out[par].sem, 16)
                pool.dma_start(v_prompt[l, 0, :, h].rearrange("(t p) e -> p t e", p=P),
                               ZH[par][:, 0:2, vcol]).then_inc(kv_out[par].sem, 16)
                pool.dma_start(k_sample[l, 0, :, h].rearrange("p m d -> p (m d)"),
                               ZH[par][0:DEC_SEQ, 2, kcol]).then_inc(kv_out[par].sem, 16)
                pool.dma_start(v_sample[l, 0, :, h], ZH[par][0:DEC_SEQ, 2, vcol]).then_inc(kv_out[par].sem, 16)
                pool.wait_ge(*kv_out[par].at(l, h_before * 4 + 4))
                pool.sem_inc(kv_stored.sem, 1)

            table_u = peer_u.rearrange("l e d -> (l e) d")
            table_v = peer_v.rearrange("l e d -> (l e) d")

            def gathers(l, b, par):
                pool.wait_ge(*idx_staged.at(l, b + 1))
                for s in range(BATCH):
                    pool.wait_ge(*u_free.at(l, b * BATCH + (s + 1 - BATCH)))
                    pool.nop(nofuse=True)
                    pool.indirect_dma_start(RING_U[:, s, :], None, table_u,
                                            bass.IndirectOffsetOnAxis(STI[:, par, s:s + 1], 0))\
                        .then_inc(u_in[s].sem, 16)
                for s in range(BATCH):
                    pool.wait_ge(*v_free.at(l, b * BATCH + (s + 1 - BATCH)))
                    pool.nop(nofuse=True)
                    pool.indirect_dma_start(RING_V[:, s, :], None, table_v,
                                            bass.IndirectOffsetOnAxis(STI[:, par, s:s + 1], 0))\
                        .then_inc(v_in[s].sem, 16)

            with pool.Fori(0, DEPTH) as l:
                pool.wait_ge(*so_sb.at(l, 1))
                for dst, at, n in ((conv_prompt[l, 0], ST_CP, CONV_HIST), (pool_prompt[l, 0], ST_PP, POOL_HIST),
                                   (conv_sample[l, 0], ST_CS, CONV_HIST), (pool_sample[l, 0], ST_PS, POOL_HIST),
                                   (lru_prompt[l], ST_LP, 1), (lru_sample[l], ST_LS, 1)):
                    pool.dma_start(dst, SOT[at:at + n, :]).then_inc(so_out.sem, 16)
                with pool.Fori(0, HEADS // 2) as g:
                    for par in range(2):
                        rotary(l, g, par)
                b0 = 0
                for t in range(TILES):
                    with pool.Fori(0, TILE_B[t] // 2) as g:
                        for par in range(2):
                            gathers(l, g * 2 + (b0 + par), par)
                    b0 += TILE_B[t]
                pool.wait_ge(*so_out.at(l, 6))
                pool.nop(nofuse=True)
                pool.drain().then_inc(layer_done.sem, 1)
                pool.wait_ge(*layer_done.at(l, 4))

        @block.tensor
        def _(pe):
            pe.wait_ge(setup.sem, 17)

            def norm_turn(l, n0):
                pe.wait_ge(*hn_ready.at(l, n0 // KC + 1))
                for c in range(KC):
                    if n0 + c >= 2:
                        pe.wait_ge(*nt_ev.at(l, n0 + c - 1))
                    for t in range(TILES):
                        i = pe.transpose(bank(2 + c % 2, t * P, (t + 1) * P), HN[:, t, c * P:(c + 1) * P],
                                         ident[:, :])
                    i.then_inc(nt_ps.sem, 1)

            def qkv(l, h, par, tiles):
                for t in tiles:
                    if t == 0:
                        pe.wait_ge(*qkv_in[par].at(l, (h - par) // 2 * 3 + 3) if isinstance(h, int)
                                   else (qkv_in[par].sem, (l * (3 * HEADS // 2) + (h[0] * 3 + 3)) * 16))
                    n = None
                    hh = h if isinstance(h, int) else h[0] * 2 + h[1]
                    b = (par * TILES + t) % 2
                    if not (isinstance(h, int) and h == 0 and t < 2):
                        pe.wait_ge(*z_ev.at(l, hh * TILES + (t - 1)))
                    for c in range(KC):
                        i = pe.matmul(bank(b, 0, 3 * HW), HT[:, c, t * P:(t + 1) * P], WQKV[par][:, c, :],
                                      start=c == 0, stop=c == KC - 1)
                    i.then_inc(z_ps.sem, 1)
                    if t == TILES - 1:
                        pe.drain().then_inc(qkv_used[par].sem, 1)

            def head(l, g, par, nxt):
                h = g * 2 + par
                z = ZH[par]
                pe.wait_ge(*rot_done.at(l, h * 2 + 2))
                pe.wait_ge(*ex_done.at(l, h * 2 * TILES))
                for t in range(TILES):
                    i = pe.transpose(bank(2, t * P, (t + 1) * P), z[:, t, 0:HW], ident[:, :])
                i.then_inc(qt_ps.sem, 1)
                pe.wait_ge(*pta_ev.at(l, h))
                for t in range(TILES):
                    pe.transpose(bank(3, t * P, (t + 1) * P), z[:, t, HW:2 * HW], ident[:, :])
                pe.wait_ge(cache_in[par].sem, (l * HEADS + (g * 2 + 2)) * 16)
                for t in range(2):
                    i = pe.transpose(bank(5, t * P, (t + 1) * P), CK[par][:, t, :], ident[:, :])
                i.then_inc(kt_ps.sem, 1)
                if nxt:
                    qkv(l, nxt, 1 - par, [0])
                pe.wait_ge(*qt_ev.at(l, h * 2 + 2))
                pe.wait_ge(*kt_ev.at(l, h + 1))
                pe.wait_ge(*ptb_ev.at(l, h))
                for t in range(2):
                    n = (t + 1) * P
                    for m in range(2):
                        out = bank(4 if t == 0 else 6, m * n, (m + 1) * n)
                        pe.matmul(out, QT[:, m, t * P:(t + 1) * P], KT[:, 0:n], start=True, stop=False)
                        mk = mask_k[:, 1, :] if t == 0 else mask_k[:, :, :].rearrange("p a b -> p (a b)")
                        i = pe.matmul(out, mask_q[:, :], mk, start=False, stop=True)
                    i.then_inc(s_ps.sem, 1)
                for m in range(2):
                    i = pe.matmul(bank(5 if m == 0 else 2, 0, PAST + DEC_SEQ), QT[:, m, 2 * P:3 * P],
                                  KT[:, SEQ:SEQ + PAST + DEC_SEQ], start=True, stop=True)
                i.then_inc(s_ps.sem, 1)
                if nxt:
                    qkv(l, nxt, 1 - par, [1, 2])
                for t in range(2):
                    pe.wait_ge(*p_ready.at(l, h * TILES + t + 1))
                    for c in range(t + 1):
                        i = pe.transpose(bank(3, (t + c) * P, (t + c + 1) * P), PC[t][:, c * P:(c + 1) * P],
                                         ident[:, :])
                i.then_inc(pta_ps.sem, 1)
                pe.wait_ge(*p_ready.at(l, h * TILES + 3))
                for c in range(3):
                    i = pe.transpose(bank(4, c * P, (c + 1) * P), PC[2][:, c * P:(c + 1) * P], ident[:, :])
                i.then_inc(ptb_ps.sem, 1)
                pe.wait_ge(*o_ev.at(l, h))
                pe.wait_ge(*pta_ev.at(l, h + 1))
                v = [z[:, t, 2 * HW:3 * HW] for t in range(TILES)]
                pe.matmul(bank(7, 0, P), PTA[:, 0:P], v[0], start=True, stop=True)
                pe.matmul(bank(7, P, 2 * P), PTA[:, P:2 * P], v[0], start=True, stop=False)
                pe.matmul(bank(7, P, 2 * P), PTA[:, 2 * P:3 * P], v[1], start=False, stop=True)
                pe.wait_ge(*ptb_ev.at(l, h + 1))
                for c, vv in enumerate((CV[par][:, 0, :], CV[par][:, 1, :], v[2])):
                    i = pe.matmul(bank(7, 2 * P, 3 * P), PTB[:, c * P:(c + 1) * P], vv,
                                  start=c == 0, stop=c == 2)
                i.then_inc(att_done.sem, 1)
                pe.drain().then_inc(cache_free.sem, 1)

            def experts(l, b, par, t):
                for s in range(BATCH):
                    pe.wait_ge(*dg_ready.at(l, b * BATCH + s + 1))
                    pe.wait_ge(*v_in[s].at(l, b + 1))
                    for j in range(2):
                        i = pe.matmul(bank(2 * (t % 2) + j), DG[:, s, :], RING_V[:, s, j * 512:(j + 1) * 512],
                                      start=False, stop=False, skip_group_check=True)
                    i.then_inc(v_free.sem, 1)

            with pe.Fori(0, DEPTH) as l:
                pe.wait_ge(*small_in.at(l, NSMALL))
                for c in range(RC):
                    i = pe.transpose(bank(0, c * P, (c + 1) * P), rows[:, c * P:(c + 1) * P], ident[:, :])
                i.then_inc(par_ps.sem, 1)
                for a in range(2):
                    i = pe.transpose(bank(1, a * P, (a + 1) * P), SKR[:, a, :], ident[:, :])
                i.then_inc(par_ps.sem, 1)
                norm_turn(l, 0)
                pe.wait_ge(*nt_ev.at(l, KC))
                for u in range(3 * HB):
                    pe.wait_ge(*w_in_slot[u % SLOTS].at(l, u // SLOTS + 1))
                    for k in range(2):
                        n = 2 * u + k
                        if n >= 2:
                            pe.wait_ge(*ff_ev.at(l, n - 1))
                        for c in range(KC):
                            i = pe.matmul(bank(4 + n % 2, 0, TOK), W[:, u % SLOTS, c, k * P:(k + 1) * P],
                                          HT[:, c, 0:TOK], start=c == 0, stop=c == KC - 1)
                        i.then_inc(ff_ps.sem, 1)
                    pe.drain().then_inc(w_used[u % SLOTS].sem, 1)
                pe.wait_ge(*par_sb.at(l, 2))
                qkv(l, 0, 0, range(TILES))
                pe.wait_ge(*xc_ready.at(l, 1))
                for c in range(RC):
                    for j, wt in enumerate((BDA, BDX)):
                        if c >= 1:
                            pe.wait_ge(*sig_ev.at(l, 2 * c - 1 + j))
                        pe.matmul(bank(6 + j, 0, XC_W), wt[:, c, :], XC[:, c, :],
                                  start=True, stop=True).then_inc(bd_ps.sem, 1)
                pe.wait_ge(*d_ready.at(l, 1))
                pe.wait_ge(*ff_ev.at(l, 12))
                for c in range(RC):
                    if c >= 2:
                        pe.wait_ge(*pl_ev.at(l, c - 1))
                    for a, n, at in POOL_PARTS:
                        i = pe.matmul(bank(4 + c % 2, at, at + n), POOLW[:, c, :], SUMS[c][:, a:a + n],
                                      start=True, stop=True)
                    i.then_inc(pl_ps.sem, 1)
                pe.wait_ge(*so_ready.at(l, 1))
                pe.wait_ge(*sig_ev.at(l, 2 * RC))
                for c in range(RC):
                    i = pe.transpose(bank(6, c * P, (c + 1) * P), SO[:, c, :], ident[:, :])
                i.then_inc(so_ps.sem, 1)
                pe.wait_ge(*pl_ev.at(l, RC))
                pe.wait_ge(*so_sb.at(l, 1))
                pe.nop(nofuse=True)
                with pe.Fori(0, HEADS // 2 - 1) as g:
                    head(l, g, 0, (g, 1))
                    head(l, g, 1, (g + 1, 0))
                head(l, HEADS // 2 - 1, 0, (HEADS // 2 - 1, 1))
                head(l, HEADS // 2 - 1, 1, None)
                pe.wait_ge(*on_ready.at(l, 1))
                for hh in range(HEADS):
                    if hh >= 2:
                        pe.wait_ge(*yt_ev.at(l, hh - 1))
                    for t in range(TILES):
                        i = pe.transpose(bank(2 + hh % 2, t * P, (t + 1) * P), OALL[:, t, hh, :], ident[:, :])
                    i.then_inc(yt_ps.sem, 1)
                pe.wait_ge(*yt_ev.at(l, HEADS))
                pe.nop(nofuse=True)
                with pe.Fori(0, GB) as g:
                    for k in range(2):
                        dc = g * 2 + k
                        cols = slice(k * P, (k + 1) * P)
                        pe.wait_ge(*sg_ev.at(l, dc * N_BRANCH))
                        for b in range(N_BRANCH):
                            if k == 0:
                                pe.wait_ge(*w_in_slot[b].at(l, g + (3 if b == 0 else 2)))
                            for c in range(KC):
                                i = pe.matmul(bank(b, 0, TOK), W[:, b, c, cols], HT[:, c, 0:TOK],
                                              start=c == 0, stop=c == KC - 1)
                            i.then_inc(gate_ps.sem, 1)
                            if k == 1:
                                pe.drain().then_inc(w_used[b].sem, 1)
                        pe.wait_ge(*m_ev.at(l, dc))
                        if k == 0:
                            pe.wait_ge(*w_in_slot[3].at(l, g + 2))
                            pe.wait_ge(*projab_in.at(l, g + 1))
                        for c in range(RC):
                            pe.matmul(bank(3, 0, TOK), W[:, 3, c, cols], YT[:, c, :],
                                      start=c == 0, stop=c == RC - 1)
                        for c in range(RC):
                            i = pe.matmul(bank(4, 0, TOK), W[:, 3, RC + c, cols], YT[:, RC + c, :],
                                          start=c == 0, stop=c == RC - 1)
                        if k == 1:
                            i.then_inc(w_used[3].sem, 1)
                        if k == 0:
                            pe.wait_ge(*w_in_slot[4].at(l, g + 2))
                        for c in range(HEADS):
                            i = pe.matmul(bank(5, 0, TOK), W[:, 4, c, cols], YT[:, 2 * RC + c, :],
                                          start=c == 0, stop=c == HEADS - 1)
                        i.then_inc(proj_ps.sem, 1)
                        if k == 1:
                            pe.drain().then_inc(w_used[4].sem, 1)
                pe.wait_ge(*mt_ready.at(l, 1))
                for u in range(GB):
                    pe.wait_ge(*w_in_slot[u].at(l, GB + (3 if u == 0 else 2)))
                    for t in range(TILES):
                        n = u * TILES + t
                        if n >= 2:
                            pe.wait_ge(*xo_ev.at(l, n - 1))
                        for c in range(KC):
                            i = pe.matmul(bank(6 + n % 2, 0, UNIT), MT[:, c, t * P:(t + 1) * P], W[:, u, c, :],
                                          start=c == 0, stop=c == KC - 1)
                        i.then_inc(xo_ps.sem, 1)
                    pe.drain().then_inc(w_used[u].sem, 1)
                norm_turn(l, KC)
                pe.wait_ge(*nt_ev.at(l, 2 * KC))
                pe.nop(nofuse=True)
                with pe.Fori(0, 2) as g:
                    def key_scores(n):
                        pe.wait_ge(*pq_ev.at(l, g * 8 + n + 1))
                        pe.wait_ge(*sc_ev.at(l, g * 8 + max(n - 1, 0)))
                        for t in range(TILES):
                            i = pe.matmul(bank(4 + n % 2, t * P, (t + 1) * P), QS[:, n % 2, t * P:(t + 1) * P],
                                          SKT[:, n % 2, :], start=True, stop=True)
                        i.then_inc(sc_ps.sem, 1)

                    for n in range(8):
                        j, k = n // 2, n % 2
                        if k == 0:
                            pe.wait_ge(*w_in_slot[j].at(l, g + GB + (4 if j == 0 else 3)))
                        for c in range(KC):
                            i = pe.matmul(bank(n % 2, 0, TOKD), W[:, j, c, k * P:(k + 1) * P], HT[:, c, :],
                                          start=c == 0, stop=c == KC - 1)
                        i.then_inc(pq_ps.sem, 1)
                        if k == 1:
                            pe.drain().then_inc(w_used[j].sem, 1)
                        if n:
                            key_scores(n - 1)
                    key_scores(7)
                b0 = 0
                for t in range(TILES):
                    pe.wait_ge(*acc_clear.at(l, t + 1))
                    pe.nop(nofuse=True)
                    with pe.Fori(0, TILE_B[t] // 2) as g:
                        for par in range(2):
                            experts(l, g * 2 + (b0 + par), par, t)
                    b0 += TILE_B[t]
                pe.drain().then_inc(layer_done.sem, 1)
                pe.wait_ge(*layer_done.at(l, 4))

        @block.scalar
        def _(act):
            act.wait_ge(setup.sem, 17)
            act.wait_ge(loaded_x.sem, 5 * 16)

            def squares(n):
                for t in range(TILES):
                    act.activation(SQ_OUT(t), X[:, t, :], ACT.Square, accum_out=ss[:, t:t + 1])
                act.drain()
                act.activation(sd[:, :], ss[:, :], ACT.Sqrt, bias=eps_c[:, :], scale=1.0 / D_MODEL)\
                    .then_inc(sq_done.sem, 1)

            def SQ_OUT(t):
                return HN[:, t, :]

            def turned(l, n0):
                for c in range(KC):
                    act.wait_ge(*nt_ps.at(l, n0 + c + 1))
                    act.activation(HT[:, c, :], bank(2 + c % 2, 0, TOKD), ACT.Copy).then_inc(nt_ev.sem, 1)

            def z_out(l, g, par, tiles):
                h = g * 2 + par
                for t in tiles:
                    if t == 0 and not (isinstance(g, int) and g == 0):
                        act.wait_ge(*att_done.at(l, g * 2 + (par - 1)))
                        act.wait_ge(*kv_stored.at(l, g * 2 + (par - 1)))
                    act.wait_ge(*z_ps.at(l, h * TILES + t + 1))
                    act.activation(ZH[par][:, t, :], bank((par * TILES + t) % 2, 0, 3 * HW), ACT.Copy)\
                        .then_inc(z_ev.sem, 1)

            def head(l, g, par, nxt):
                h = g * 2 + par
                act.wait_ge(*qt_ps.at(l, h + 1))
                for m in range(2):
                    d = slice(m * HD, (m + 1) * HD)
                    act.activation(QT[d, m, :], bank(2, 0, TOKD)[d], ACT.Copy).then_inc(qt_ev.sem, 1)
                if nxt is not None:
                    z_out(l, *nxt, [0])
                for t in range(TILES):
                    act.wait_ge(*nb_ready.at(l, h * TILES + t + 1))
                    n = P * (t + 1) if t < 2 else PAST + DEC_SEQ
                    for m in range(2):
                        src = (bank(4, m * n, (m + 1) * n), bank(6, m * n, (m + 1) * n),
                               bank(5 if m == 0 else 2, 0, n))[t]
                        act.activation(PR[t][:, m, :], src, ACT.Exp, bias=nb[:, t, m:m + 1], scale=SCALE,
                                       accum_out=sme[:, t, m:m + 1]).then_inc(ex_done.sem, 1)
                if nxt is not None:
                    z_out(l, *nxt, [1, 2])
                act.wait_ge(*pta_ps.at(l, h + 1))
                act.activation(PTA, bank(3, 0, 3 * P), ACT.Copy).then_inc(pta_ev.sem, 1)

            def exponents(l, n):
                act.wait_ge(*best_ready.at(l, n + 1))
                act.activation(GEX[:, :], BSM[:, :], ACT.Exp, accum_out=GSM[:, :]).then_inc(gex_ready.sem, 1)

            def weights(l, b, t):
                act.wait_ge(*av_ready.at(l, b + 1))
                act.activation(GV[:, :], AV[:, :], ACT.Gelu).then_inc(gv_ready.sem, 1)
                act.wait_ge(*wv_ready.at(l, b + 1))
                for s in range(BATCH):
                    act.wait_ge(*v_free.at(l, b * BATCH + (s + 1 - BATCH)))
                    act.activation(DG[:, s, :], (twins if t == 2 else ident)[:, :], ACT.Copy,
                                   scale=WV[:, s:s + 1]).then_inc(dg_ready.sem, 1)

            with act.Fori(0, DEPTH) as l:
                squares(0)
                turned(l, 0)
                act.wait_ge(*lam_dot.at(l, 1))
                act.activation(LE[:, :], LD[:, :], ACT.Exp).then_inc(lam_exp.sem, 1)
                act.wait_ge(*sp_in.at(l, 1))
                act.activation(spt[:, 1, :], spt[:, 0, :], ACT.Exp)
                act.drain()
                act.activation(spt[:, 2, :], spt[:, 1, :], ACT.Ln, bias=1.0).then_inc(sp_ln.sem, 1)
                for u in range(3 * HB):
                    kind, j = u % 3, u // 3
                    for k in range(2):
                        n, c = 2 * u + k, 2 * j + k
                        act.wait_ge(*ff_ps.at(l, n + 1))
                        src = bank(4 + n % 2, 0, TOK)
                        if kind == 1:
                            i = act.activation(YT[:, c, :], src, ACT.Gelu)
                        else:
                            buf, h0, s0 = ((XA, CONV_HIST, XA_S + CONV_HIST), None,
                                           (XQ, POOL_HIST, XQ_S + POOL_HIST))[kind]
                            act.activation(buf[:, c, h0:h0 + SEQ], src[:, 0:SEQ], ACT.Copy)
                            i = act.activation(buf[:, c, s0:s0 + DEC_SEQ], src[:, SEQ:TOK], ACT.Copy)
                        act.drain().then_inc(ff_ev.sem, 1)
                z_out(l, 0, 0, range(TILES))
                act.wait_ge(*par_sb.at(l, 2))
                for c in range(RC):
                    for j, (dst, row) in enumerate(((RG, "lru_ba"), (IG, "lru_bx"))):
                        act.wait_ge(*bd_ps.at(l, 2 * c + j + 1))
                        act.activation(dst[:, c, :], bank(6 + j, 0, XC_W), ACT.Sigmoid,
                                       bias=PT[:, c, ROW[row]:ROW[row] + 1]).then_inc(sig_ev.sem, 1)
                act.wait_ge(*sp_out.at(l, 1))
                act.nop(nofuse=True)
                act.drain()
                for c in range(RC):
                    act.activation(DEC[:, c, :], RG[:, c, :], ACT.Exp, scale=nsp[:, c:c + 1])
                act.drain()
                for c in range(RC):
                    act.activation(RG[:, c, :], RG[:, c, :], ACT.Tanh, scale=nsp[:, c:c + 1])
                act.drain().then_inc(decay.sem, 1)
                for c in range(RC):
                    act.wait_ge(*pl_ps.at(l, c + 1))
                    act.activation(YT[:, RC + c, :], bank(4 + c % 2, 0, TOK), ACT.Copy,
                                   scale=PT[:, c, ROW["pool_scale"]:ROW["pool_scale"] + 1])\
                        .then_inc(pl_ev.sem, 1)
                act.wait_ge(*oma.at(l, 1))
                act.activation(RG[:, :, :], RG[:, :, :], ACT.Sqrt).then_inc(root.sem, 1)
                with act.Fori(0, HEADS // 2 - 1) as g:
                    head(l, g, 0, (g, 1))
                    head(l, g, 1, (g + 1, 0))
                head(l, HEADS // 2 - 1, 0, (HEADS // 2 - 1, 1))
                head(l, HEADS // 2 - 1, 1, None)
                act.wait_ge(*sso_ready.at(l, 1))
                act.activation(rso[:, :, :], sso[:, :, :], ACT.Sqrt, bias=eps_c[:, :], scale=1.0 / HW)\
                    .then_inc(sso_root.sem, 1)
                for hh in range(HEADS):
                    act.wait_ge(*yt_ps.at(l, hh + 1))
                    act.activation(YT[:, 2 * RC + hh, :], bank(2 + hh % 2, 0, TOK), ACT.Copy)\
                        .then_inc(yt_ev.sem, 1)
                with act.Fori(0, GB) as g:
                    for k in range(2):
                        dc = g * 2 + k
                        act.wait_ge(*m_ev.at(l, dc))
                        for b in range(N_BRANCH):
                            act.wait_ge(*gate_ps.at(l, dc * N_BRANCH + b + 1))
                            act.activation(SG[:, b, :], bank(b, 0, TOK), ACT.Sigmoid).then_inc(sg_ev.sem, 1)
                act.wait_ge(*xo_ev.at(l, GB * TILES))
                squares(1)
                turned(l, KC)
                with act.Fori(0, 2) as g:
                    for n in range(8):
                        act.wait_ge(*pq_ps.at(l, g * 8 + n + 1))
                        act.activation(QS[:, n % 2, :], bank(n % 2, 0, TOKD), ACT.Copy).then_inc(pq_ev.sem, 1)
                exponents(l, 0)
                for t in range(2):
                    with act.Fori(0, PH) as h:
                        weights(l, h * 2 + t * TILE_B[0], t)
                        exponents(l, h + (t * PH + 1))
                        weights(l, h * 2 + (t * TILE_B[0] + 1), t)
                with act.Fori(0, PH - 1) as h:
                    exponents(l, h + (2 * PH + 1))
                    weights(l, h + 2 * TILE_B[0], 2)
                weights(l, BATCHES - 1, 2)
                act.drain().then_inc(layer_done.sem, 1)
                act.wait_ge(*layer_done.at(l, 4))
            squares(2)

        @block.vector
        def _(dve):
            dve.wait_ge(setup.sem, 17)
            dve.wait_ge(loaded_x.sem, 5 * 16)

            def fence():
                dve.drain()

            def normed(n, sem, val):
                dve.wait_ge(*val)
                dve.reciprocal(rstd[:, :], sd[:, :])
                fence()
                dve.wait_ge(*sem)
                for t in range(TILES):
                    dve.scalar_tensor_tensor(out=HN[:, t, :], in0=X[:, t, :], scalar=rstd[:, t:t + 1],
                                             in1=G[:, :], op0=ALU.mult, op1=ALU.mult)

            def head(l, g, par):
                h = g * 2 + par
                dve.wait_ge(*kt_ps.at(l, h + 1))
                dve.tensor_copy(KT[:, 0:SEQ], bank(3, 0, SEQ))
                dve.tensor_copy(KT[:, 2 * SEQ:2 * SEQ + P], bank(3, SEQ, SEQ + P))
                dve.tensor_copy(KT[:, SEQ:2 * SEQ], bank(5, 0, PAST))
                dve.drain().then_inc(kt_ev.sem, 1)
                for t in range(TILES):
                    dve.wait_ge(*s_ps.at(l, h * TILES + t + 1))
                    if t < 2:
                        n = P * (t + 1)
                        dve.tensor_reduce(mxs[:, t, :], bank(4 if t == 0 else 6, 0, 2 * n)
                                          .rearrange("p (m k) -> p m k", m=2), AX_X, ALU.max)
                    else:
                        for m in range(2):
                            dve.tensor_reduce(mxs[:, t, m:m + 1], bank(5 if m == 0 else 2, 0, PAST + DEC_SEQ),
                                              AX_X, ALU.max)
                    fence()
                    dve.tensor_scalar(nb[:, t, :], mxs[:, t, :], -SCALE, None, ALU.mult)\
                        .then_inc(nb_ready.sem, 1)
                for t in range(TILES):
                    n = P * (t + 1) if t < 2 else PAST + DEC_SEQ
                    dve.wait_ge(*ex_done.at(l, h * 2 * TILES + 2 * t + 2))
                    dve.reciprocal(rec[:, t, :], sme[:, t, :])
                    fence()
                    dve.tensor_tensor(rec[:, t, 1:2], rec[:, t, 1:2], neg_lam[:, :], ALU.mult)
                    dve.tensor_scalar(PC[t][:, 0:n], PR[t][:, 0, :], rec[:, t, 0:1], None, ALU.mult)
                    fence()
                    dve.scalar_tensor_tensor(out=PC[t][:, 0:n], in0=PR[t][:, 1, :], scalar=rec[:, t, 1:2],
                                             in1=PC[t][:, 0:n], op0=ALU.mult, op1=ALU.add)
                    dve.drain().then_inc(p_ready.sem, 1)
                dve.wait_ge(*ptb_ps.at(l, h + 1))
                dve.tensor_copy(PTB[:, :], bank(4, 0, 3 * P)).then_inc(ptb_ev.sem, 1)
                dve.wait_ge(*att_done.at(l, h + 1))
                dve.tensor_copy(OALL[:, :, h, :], bank(7, 0, 3 * P).rearrange("p (t e) -> p t e", t=TILES))\
                    .then_inc(o_ev.sem, 1)

            def route(l, t, h):
                dve.tensor_copy(STG, SALL[:, t, bass.ds(h * 2, 2), :] if not isinstance(h, int)
                                else SALL[:, t, 2 * h:2 * h + 2, :])
                fence()
                for a in range(2):
                    dve.max(out=MX[:, a, 0:8], in_=STG[:, a, :])
                fence()
                for a in range(2):
                    dve.match_replace(out=STG2[:, a, :], in_to_replace=MX[:, a, 0:8], in_values=STG[:, a, :],
                                      imm_value=LOW)
                    dve.max_index(out=IX[:, a, 0:8], in_max=MX[:, a, 0:8], in_values=STG[:, a, :])
                fence()
                for a in range(2):
                    dve.max(out=MX[:, a, 8:16], in_=STG2[:, a, :])
                fence()
                for a in range(2):
                    dve.max_index(out=IX[:, a, 8:16], in_max=MX[:, a, 8:16], in_values=STG2[:, a, :])
                dve.tensor_tensor(CAND, MX[:, 0, :].unsqueeze(2).to_broadcast([P, TOPK, TOPK]),
                                  MX[:, 1, :].unsqueeze(1).to_broadcast([P, TOPK, TOPK]), ALU.add)
                fence()
                flat, flat2 = (x.rearrange("p a b -> p (a b)") for x in (CAND, CAND2))
                dve.max(out=BS[:, 0:8], in_=flat)
                dve.tensor_copy(IXF[:, :, :], IX[:, :, :])
                fence()
                dve.match_replace(out=flat2, in_to_replace=BS[:, 0:8], in_values=flat, imm_value=LOW)
                dve.max_index(out=BC[:, 0:8], in_max=BS[:, 0:8], in_values=flat)
                fence()
                dve.max(out=BS[:, 8:16], in_=flat2)
                fence()
                dve.max_index(out=BC[:, 8:16], in_max=BS[:, 8:16], in_values=flat2)
                dve.tensor_scalar(BSM[:, :], BS[:, :], BS[:, 0:1], None, ALU.subtract)\
                    .then_inc(best_ready.sem, 1)
                fence()
                dve.tensor_scalar(CI[:, 0, :], BC[:, :], 4, None, ALU.logical_shift_right)
                dve.tensor_scalar(CI[:, 1, :], BC[:, :], TOPK - 1, None, ALU.bitwise_and)
                fence()
                dve.tensor_copy(CIF[:, :, :], CI[:, :, :])
                fence()
                hot = [HOT[:, a, :].rearrange("p (k j) -> p k j", k=TOPK) for a in range(2)]
                for a in range(2):
                    dve.tensor_tensor(hot[a], CIF[:, a, :].unsqueeze(2).to_broadcast([P, TOPK, TOPK]),
                                      iota16[:, :].unsqueeze(1).to_broadcast([P, TOPK, TOPK]), ALU.is_equal)
                fence()
                for a in range(2):
                    dve.tensor_tensor(hot[a], hot[a], IXF[:, a, :].unsqueeze(1).to_broadcast([P, TOPK, TOPK]),
                                      ALU.mult)
                fence()
                for a in range(2):
                    dve.tensor_reduce(I12[:, a, :], hot[a], AX_X, ALU.add)
                fence()
                dve.scalar_tensor_tensor(out=IDF[:, :], in0=I12[:, 0, :], scalar=float(NK), in1=I12[:, 1, :],
                                         op0=ALU.mult, op1=ALU.add)
                fence()
                dve.tensor_scalar(IDX[:, :], IDF[:, :], LCON[:, 2:3], None, ALU.add)
                fence()

            def gates(l, n):
                dve.wait_ge(*gex_ready.at(l, n + 1))
                dve.reciprocal(GRC[:, :], GSM[:, :])
                fence()
                dve.tensor_scalar(GATE[:, :], GEX[:, :], GRC[:, :], None, ALU.mult)
                fence()

            def halves(t, k):
                if t < 2:
                    return [(slice(0, P), slice(k * BATCH, (k + 1) * BATCH))]
                return [(slice(i * CHUNK, (i + 1) * CHUNK), slice(i * BATCH, (i + 1) * BATCH)) for i in range(2)]

            def stage(l, b, par, t, k):
                dve.wait_ge(*v_free.at(l, (b - 1) * BATCH if not isinstance(b, int) or b >= 1 else 0))
                for r, c in halves(t, k):
                    dve.tensor_copy(STI[r, par, :], IDX[r, c])
                dve.drain().then_inc(idx_staged.sem, 1)

            def dots(l, b, t):
                for s in range(BATCH):
                    dve.wait_ge(*u_in[s].at(l, b + 1))
                    dve.tensor_tensor_reduce(RING_U[:, s, :], RING_U[:, s, :], HN[:, t, :], 1.0, 0.0,
                                             ALU.mult, ALU.add, AV[:, s:s + 1]).then_inc(u_free.sem, 1)
                dve.drain().then_inc(av_ready.sem, 1)

            def weigh(l, b, t, k):
                dve.wait_ge(*gv_ready.at(l, b + 1))
                for r, c in halves(t, k):
                    dve.tensor_tensor(WV[r, :], GV[r, :], GATE[r, c], ALU.mult)
                dve.drain().then_inc(wv_ready.sem, 1)

            def two_batches(l, h, t, then):
                b = h * 2 + t * TILE_B[0]
                gates(l, h + t * PH)
                dots(l, b, t)
                stage(l, b + 1, 1, t, 1)
                weigh(l, b, t, 0)
                route(l, *then)
                dots(l, b + 1, t)
                stage(l, b + 2, 0, then[0], 0)
                weigh(l, b + 1, t, 1)

            def one_batch(l, h, par, then):
                b = h + 2 * TILE_B[0]
                gates(l, h + 2 * PH)
                if then:
                    route(l, *then)
                    stage(l, b + 1, 1 - par, 2, 0)
                dots(l, b, 2)
                weigh(l, b, 2, 0)

            def clear(t):
                dve.memset(ps[:, 1024 * (t % 2):1024 * (t % 2 + 1)], 0.0).then_inc(acc_clear.sem, 1)

            def add_experts(l, t):
                dve.wait_ge(*v_free.at(l, sum(TILE_B[:t + 1]) * BATCH))
                dve.tensor_tensor(X[:, t, :], X[:, t, :], ps[:, 1024 * (t % 2):1024 * (t % 2 + 1)], ALU.add)

            with dve.Fori(0, DEPTH) as l:
                normed(0, gain_in.at(l, 1), sq_done.at(l, 1))
                dve.drain().then_inc(hn_ready.sem, 1)
                dve.drain().then_inc(gain_used.sem, 1)
                dve.wait_ge(*small_in.at(l, NSMALL))
                for a in range(2):
                    dve.tensor_tensor_reduce(LAMV[:, 2 * a, :], LAMV[:, 2 * a, :], LAMV[:, 2 * a + 1, :], 1.0, 0.0,
                                             ALU.mult, ALU.add, LD[:, a:a + 1])
                dve.tensor_scalar(SUBG[:, :], SUBG[:, :], LCON[:, 1:2], None, ALU.mult)
                dve.drain().then_inc(lam_dot.sem, 1)
                dve.wait_ge(*par_ps.at(l, 1))
                dve.tensor_copy(PT[:, :, :], bank(0).rearrange("p (c r) -> p c r", c=RC)[:, :, 0:NROW])\
                    .then_inc(par_sb.sem, 1)
                dve.wait_ge(*par_ps.at(l, 2))
                dve.tensor_copy(SKT[:, :, :], bank(1, 0, 2 * NK).rearrange("p (a k) -> p a k", a=2))\
                    .then_inc(par_sb.sem, 1)
                fence()
                L = PT[:, :, ROW["lru_L"]]
                dve.tensor_scalar(nsp[:, :], L, -1.0, 0.0, ALU.mult, ALU.max)
                dve.tensor_scalar(spt[:, 1, :], L, -1.0, None, ALU.mult)
                fence()
                dve.tensor_tensor(spt[:, 0, :], L, spt[:, 1, :], ALU.min)
                dve.drain().then_inc(sp_in.sem, 1)
                dve.wait_ge(*lam_exp.at(l, 1))
                dve.tensor_tensor(neg_lam[:, :], LE[:, 1:2], LE[:, 0:1], ALU.subtract)
                fence()
                dve.tensor_tensor(neg_lam[:, :], neg_lam[:, :], LCON[:, 0:1], ALU.subtract)
                dve.wait_ge(*sp_ln.at(l, 1))
                dve.tensor_tensor(nsp[:, :], nsp[:, :], spt[:, 2, :], ALU.add)
                fence()
                dve.tensor_scalar(nsp[:, :], nsp[:, :], -LRU_C, None, ALU.mult).then_inc(sp_out.sem, 1)
                dve.memset(XA[:, :, 0:CONV_HIST], 0.0)
                dve.memset(XQ[:, :, 0:POOL_HIST], 0.0)
                dve.tensor_copy(XA[:, :, XA_S:XA_S + CONV_HIST],
                                PT[:, :, ROW["conv_state"]:ROW["conv_state"] + CONV_HIST])
                dve.tensor_copy(XQ[:, :, XQ_S:XQ_S + POOL_HIST],
                                PT[:, :, ROW["pool_state"]:ROW["pool_state"] + POOL_HIST])
                dve.wait_ge(*ff_ev.at(l, 8))
                dve.nop(nofuse=True)
                fence()
                for j in range(CONV_W):
                    for c in range(RC):
                        w = PT[:, c, ROW["conv_w"] + j:ROW["conv_w"] + j + 1]
                        if j == 0:
                            dve.tensor_scalar(XC[:, c, :], XA[:, c, 0:XC_W], w,
                                              PT[:, c, ROW["conv_b"]:ROW["conv_b"] + 1], ALU.mult, ALU.add)
                        else:
                            dve.scalar_tensor_tensor(out=XC[:, c, :], in0=XA[:, c, j:j + XC_W], scalar=w,
                                                     in1=XC[:, c, :], op0=ALU.mult, op1=ALU.add)
                    fence()
                dve.drain().then_inc(xc_ready.sem, 1)
                dve.tensor_copy(SO[:, :, ST_CP:ST_CP + CONV_HIST], XA[:, :, SEQ:SEQ + CONV_HIST])
                dve.tensor_copy(SO[:, :, ST_CS:ST_CS + CONV_HIST], XA[:, :, XA_W - CONV_HIST:XA_W])
                dve.wait_ge(*ff_ev.at(l, 12))
                dve.tensor_tensor(S1[:, :, 1:XQ_W], XQ[:, :, 1:XQ_W], XQ[:, :, 0:XQ_W - 1], ALU.add)
                fence()
                dve.tensor_tensor(S2[:, 1:4, 3:XQ_W], S1[:, 1:4, 3:XQ_W], S1[:, 1:4, 1:XQ_W - 2], ALU.add)
                fence()
                dve.tensor_tensor(S1[:, 2:4, 7:XQ_W], S2[:, 2:4, 7:XQ_W], S2[:, 2:4, 3:XQ_W - 4], ALU.add)
                fence()
                dve.tensor_tensor(S2[:, 3, 15:XQ_W], S1[:, 3, 15:XQ_W], S1[:, 3, 7:XQ_W - 8], ALU.add)
                fence()
                for c in range(RC):
                    for a, n, at in POOL_PARTS:
                        dve.tensor_tensor(SUMS[c][:, a:a + n], SUMS[c][:, a:a + n], PINV[:, c, at:at + n], ALU.mult)
                fence()
                for c in range(RC):
                    for a, n, at in POOL_PARTS:
                        dve.tensor_tensor(SUMS[c][:, a:a + n], SUMS[c][:, a:a + n], XQ[:, c, a:a + n], ALU.subtract)
                dve.drain().then_inc(d_ready.sem, 1)
                dve.wait_ge(*decay.at(l, 1))
                dve.tensor_scalar(XA[:, :, 0:XC_W], RG[:, :, :], -1.0, 1.0, ALU.mult, ALU.add)
                fence()
                dve.reciprocal(XA[:, :, 0:XC_W], XA[:, :, 0:XC_W])
                fence()
                dve.scalar_tensor_tensor(out=RG[:, :, :], in0=RG[:, :, :], scalar=-2.0, in1=XA[:, :, 0:XC_W],
                                         op0=ALU.mult, op1=ALU.mult)
                dve.drain().then_inc(oma.sem, 1)
                dve.tensor_tensor(IG[:, :, :], IG[:, :, :], XC[:, :, :], ALU.mult)
                dve.wait_ge(*root.at(l, 1))
                dve.nop(nofuse=True)
                fence()
                dve.tensor_tensor(IG[:, :, :], IG[:, :, :], RG[:, :, :], ALU.mult)
                fence()
                s0 = SEQ + CONV_HIST
                for c in range(RC):
                    dve.tensor_tensor_scan(RG[:, c, 0:SEQ], DEC[:, c, 0:SEQ], IG[:, c, 0:SEQ], 0.0,
                                           ALU.mult, ALU.add)
                    dve.tensor_tensor_scan(RG[:, c, s0:XC_W], DEC[:, c, s0:XC_W], IG[:, c, s0:XC_W],
                                           PT[:, c, ROW["lru_state"]:ROW["lru_state"] + 1],
                                           ALU.mult, ALU.add)
                fence()
                dve.tensor_tensor(YT[:, 0:RC, 0:SEQ], YT[:, 0:RC, 0:SEQ], RG[:, :, 0:SEQ], ALU.mult)
                dve.tensor_tensor(YT[:, 0:RC, SEQ:TOK], YT[:, 0:RC, SEQ:TOK], RG[:, :, s0:XC_W], ALU.mult)
                dve.tensor_copy(SO[:, :, ST_PP:ST_PP + POOL_HIST], XQ[:, :, SEQ:SEQ + POOL_HIST])
                dve.tensor_copy(SO[:, :, ST_PS:ST_PS + POOL_HIST], XQ[:, :, XQ_W - POOL_HIST:XQ_W])
                dve.tensor_copy(SO[:, :, ST_LP:ST_LP + 1], RG[:, :, SEQ - 1:SEQ])
                dve.tensor_copy(SO[:, :, ST_LS:ST_LS + 1], RG[:, :, XC_W - 1:XC_W])
                dve.drain().then_inc(so_ready.sem, 1)
                dve.wait_ge(*so_ps.at(l, 1))
                dve.tensor_copy(SOT[:, :], bank(6)).then_inc(so_sb.sem, 1)

                dve.memset(PC[2][:, PAST + DEC_SEQ:3 * P], 0.0)
                dve.memset(QT[HD:P, 0, :], 0.0)
                dve.memset(QT[0:HD, 1, :], 0.0)
                with dve.Fori(0, HEADS // 2) as g:
                    for par in range(2):
                        head(l, g, par)
                fence()
                dve.tensor_tensor(SQ, OALL, OALL, ALU.mult)
                fence()
                dve.tensor_reduce(sso[:, :, :], SQ, AX_X, ALU.add)
                dve.drain().then_inc(sso_ready.sem, 1)
                dve.wait_ge(*sso_root.at(l, 1))
                dve.reciprocal(sso[:, :, :], rso[:, :, :])
                fence()
                for t in range(TILES):
                    dve.tensor_tensor(OALL[:, t], OALL[:, t],
                                      sso[:, t, :].unsqueeze(2).to_broadcast([P, HEADS, HW]), ALU.mult)
                fence()
                for t in range(TILES):
                    dve.tensor_tensor(OALL[:, t], OALL[:, t],
                                      SUBG[:, :].unsqueeze(1).to_broadcast([P, HEADS, HW]), ALU.mult)
                dve.drain().then_inc(on_ready.sem, 1)
                with dve.Fori(0, GB) as g:
                    for k in range(2):
                        dc = g * 2 + k
                        m = MT[:, bass.ds(dc, 1), 0:TOK].rearrange("p a b -> p (a b)")
                        dve.wait_ge(*sg_ev.at(l, dc * N_BRANCH + N_BRANCH))
                        dve.wait_ge(*proj_ps.at(l, dc + 1))
                        for b in range(N_BRANCH):
                            dve.tensor_tensor(SG[:, b, :], SG[:, b, :], bank(3 + b, 0, TOK), ALU.mult)
                        fence()
                        dve.tensor_tensor(MTMP, SG[:, 0, :], SG[:, 1, :], ALU.add)
                        fence()
                        dve.tensor_tensor(m, MTMP, SG[:, 2, :], ALU.add).then_inc(m_ev.sem, 1)
                fence()
                dve.tensor_copy(MT[:, :, TOK:TOKD], MT[:, :, SEQ:TOK]).then_inc(mt_ready.sem, 1)
                for u in range(GB):
                    for t in range(TILES):
                        n = u * TILES + t
                        dve.wait_ge(*xo_ps.at(l, n + 1))
                        x = X[:, t, u * UNIT:(u + 1) * UNIT]
                        dve.tensor_tensor(x, x, bank(6 + n % 2, 0, UNIT), ALU.add).then_inc(xo_ev.sem, 1)
                normed(1, gain_in.at(l, 2), sq_done.at(l, 2))
                dve.drain().then_inc(hn_ready.sem, 1)
                with dve.Fori(0, 2) as g:
                    for n in range(8):
                        dve.wait_ge(*sc_ps.at(l, g * 8 + n + 1))
                        dve.tensor_copy(SALL[:, :, bass.ds(g * 8 + n, 1), :].rearrange("p t a k -> p t (a k)"),
                                        bank(4 + n % 2, 0, TILES * NK).rearrange("p (t k) -> p t k", t=TILES))\
                            .then_inc(sc_ev.sem, 1)
                fence()
                route(l, 0, 0)
                stage(l, 0, 0, 0, 0)
                for t in range(2):
                    clear(t)
                    with dve.Fori(0, PH - 1) as h:
                        two_batches(l, h, t, (t, h + 1))
                    two_batches(l, PH - 1, t, (t + 1, 0))
                    if t == 1:
                        add_experts(l, 0)
                fence()
                clear(2)
                with dve.Fori(0, PH // 2 - 1) as g:
                    one_batch(l, g * 2, 0, (2, g * 2 + 1))
                    one_batch(l, g * 2 + 1, 1, (2, g * 2 + 2))
                one_batch(l, PH - 2, 0, (2, PH - 1))
                one_batch(l, PH - 1, 1, None)
                add_experts(l, 1)
                add_experts(l, 2)
                dve.drain().then_inc(layer_done.sem, 1)
                dve.wait_ge(*layer_done.at(l, 4))
            normed(2, gain_in.at(DEPTH, 1), sq_done.at(DEPTH, 1))
            dve.drain().then_inc(y_ready.sem, 1)


_INS = ['x_prompt', 'x_sample', 'cache_k', 'cache_v', 'state_conv', 'state_lru', 'state_pool',
        'norm1_g', 'w_in', 'conv_w', 'conv_b', 'lru_wa', 'lru_ba', 'lru_wx', 'lru_bx', 'lru_L',
        'pool_w', 'pool_scale', 'lam_q1', 'lam_k1', 'lam_q2', 'lam_k2', 'subln_g',
        'proj_a', 'proj_b', 'proj_c', 'w_out', 'norm2_g', 'peer_wq', 'peer_subkeys', 'peer_u', 'peer_v',
        'final_g']
_OUTS = [(1, 256, 1024), (1, 64, 1024),
         (2, 1, 256, 8, 2, 64), (2, 1, 256, 8, 128), (2, 1, 3, 512), (2, 1, 512), (2, 1, 15, 512),
         (2, 1, 64, 8, 2, 64), (2, 1, 64, 8, 128), (2, 1, 3, 512), (2, 1, 512), (2, 1, 15, 512)]


def constants():
    pos = np.concatenate([np.arange(SEQ), PAST + np.arange(DEC_SEQ), PAST + np.arange(DEC_SEQ)])
    inv = np.float32(500000.0) ** (-np.arange(ROT, dtype=np.float32) / np.float32(ROT))
    ang = pos.astype(np.float32)[:, None] * inv.astype(np.float32)[None, :]
    rot = np.stack([np.cos(ang), np.sin(ang)], axis=1).astype(np.float32).reshape(TILES, P, 2, ROT)
    t = np.concatenate([np.arange(SEQ), PAST + np.arange(DEC_SEQ)])
    counts = np.stack([np.minimum(t + 1, w) for w in (2, 4, 8, 16)])
    pool_inv = (1.0 / counts).astype(np.float32)
    lam = [0.8 - 0.6 * np.exp(-0.3 * l) for l in range(DEPTH)]
    lc = np.array([[x, 1.0 - x, l * N_EXPERTS] for l, x in enumerate(lam)], np.float32)
    return {"rot_table": rot, "pool_inv": pool_inv, "layer_consts": lc}


def kernel(**inputs):
    import numpy as _np
    import concourse.bacc as _bacc
    from concourse import mybir as _mybir
    from concourse.bass_utils import run_bass_kernel_spmd as _run

    nc = _bacc.Bacc("TRN2", target_bir_lowering=False, num_devices=1)
    arrays, args = {}, []
    for name, a in [(n, inputs[n]) for n in _INS] + list(constants().items()):
        a = _np.ascontiguousarray(a)
        arrays[f"in_{name}_dram"] = a
        args.append(nc.dram_tensor(f"in_{name}_dram", a.shape, _mybir.dt.from_np(a.dtype), kind="ExternalInput").ap())
    for i, shape in enumerate(_OUTS):
        args.append(nc.dram_tensor(f"out_{i}_dram", shape, _mybir.dt.float32, kind="ExternalOutput").ap())
    build(nc, *args)
    r = _run(nc, [arrays], core_ids=[0])
    return tuple(r.results[0][f"out_{i}_dram"] for i in range(len(_OUTS)))
```

```python
from contextlib import ExitStack

import numpy as np

import concourse.bass as bass
from concourse import mybir

F32 = mybir.dt.float32
U32 = mybir.dt.uint32
ALU = mybir.AluOpType
ACT = mybir.ActivationFunctionType
AX_X = mybir.AxisListType.X

P = 128
DEPTH, D_MODEL, SEQ, DEC_SEQ, PAST = 2, 1024, 256, 64, 256
TOK = SEQ + DEC_SEQ
TILES = 3
TOKD = TILES * P
KC = D_MODEL // P
D_RNN = D_POOL = 512
RC = D_RNN // P
CONV_W, POOL_HIST, CHUNK = 4, 15, 64
HEADS, HD = 8, 64
HW = 2 * HD
ROT = HD // 8
N_BRANCH = 3
COL_Q = 2 * D_RNN + D_POOL
COL_G = COL_Q + 3 * HEADS * HW
PH, NK, TOPK = 8, 128, 16
N_EXPERTS = NK * NK
EPS = 1e-6
LRU_C = 8.0
FAR = -1e30
LOW = -3e38
SCALE = HD ** -0.5

CONV_HIST = CONV_W - 1
XA_S = CONV_HIST + SEQ
XA_W = XA_S + CONV_HIST + DEC_SEQ
XC_W = XA_W - CONV_HIST
XQ_S = POOL_HIST + SEQ
XQ_W = XQ_S + POOL_HIST + DEC_SEQ

ROW = dict(conv_state=0, pool_state=3, lru_state=18, conv_w=19, conv_b=23, lru_ba=24, lru_bx=25,
           lru_L=26, pool_scale=27)
NROW = 28
ST_CP, ST_PP, ST_CS, ST_PS, ST_LP, ST_LS = 0, 3, 18, 21, 36, 37

UNIT = 256
SLOTS = 5
HB = D_RNN // UNIT
GB = D_MODEL // UNIT
BATCH = 8

FIRST_B = 2 * PH
BATCHES = FIRST_B + 3 * PH

FF_UNITS = ((0, 0), (0, 1), (2, 0), (2, 1), (1, 0), (1, 1))
FF_USES = [2, 1, 1, 1, 1]
OUT_USES = [1, 1, 1, 1, 0]
FIRST_Q, NEXT_Q = (4, 0), 3
Q_USES = [1, 0, 0, PH - 2, 1]
SLOT_USES = [FF_USES[i] + GB + OUT_USES[i] + Q_USES[i] for i in range(SLOTS)]
BEFORE_Q = [FF_USES[i] + GB + OUT_USES[i] for i in range(SLOTS)]
Q_BLOCKS = 2 * PH + 2
TURNS = 2


class Signal:

    def __init__(self, sem, per_layer, unit=1, start=0):
        self.sem, self.per_layer, self.unit, self.start = sem, per_layer, unit, start

    def at(self, l, n):
        return self.sem, (l * self.per_layer + n) * self.unit + self.start


def build(nc, x_prompt, x_sample, cache_k, cache_v, state_conv, state_lru, state_pool,
          norm1_g, w_in, conv_w, conv_b, lru_wa, lru_ba, lru_wx, lru_bx, lru_L,
          pool_w, pool_scale, lam_q1, lam_k1, lam_q2, lam_k2, subln_g,
          proj_a, proj_b, proj_c, w_out, norm2_g, peer_wq, peer_subkeys, peer_u, peer_v,
          final_g, rot_table, pool_inv, layer_consts,
          y_prompt, y_sample, k_prompt, v_prompt, conv_prompt, lru_prompt, pool_prompt,
          k_sample, v_sample, conv_sample, lru_sample, pool_sample):
    ctx = ExitStack()
    with ctx:
        def sb(name, shape, dt=F32):
            return ctx.enter_context(nc.sbuf_tensor(name, shape, dt))

        started = []

        def signal(name, per_layer, unit=1, start=0):
            s = Signal(ctx.enter_context(nc.semaphore(name)), per_layer, unit, start)
            if start:
                started.append(s)
            return s

        def landing(name, per_layer):
            return signal(name, per_layer, 16)

        def parts(name, size):
            t = sb(name, [P, size])
            used = [0]

            def cut(*shape, at=None):
                n = int(np.prod(shape))
                a = used[0] if at is None else at
                assert a + n <= size, (name, a, n)
                used[0] = a + n
                v = t[:, a:a + n]
                names = "abc"[:len(shape)]
                if len(shape) > 1:
                    v = v.rearrange(f"p ({' '.join(names)}) -> p {' '.join(names)}",
                                    **{names[i]: shape[i] for i in range(len(shape))})
                return v
            return cut

        X = sb("X", [P, TILES, D_MODEL])
        HT = sb("HT", [P, KC, TOKD])
        G = sb("G", [P, D_MODEL])
        cut = parts("YT_HN", (4 + 4 + 8) * TOK)
        YT = cut(16, TOK)
        HN = cut(TILES, D_MODEL, at=0)
        DG = cut(BATCH, P)
        STG = cut(2, NK)
        STG2 = cut(2, NK)
        CAND = cut(TOPK, TOPK)
        CAND2 = cut(TOPK, TOPK)
        W = sb("W", [P, SLOTS, KC, UNIT])
        cut = parts("WQ_SALL", 2 * KC * 3 * HW)
        WQKV = cut(2, KC * 3 * HW)
        WQKV = [WQKV[:, i, :].rearrange("p (c n) -> p c n", c=KC) for i in range(2)]
        SALL = cut(TILES, 2 * PH, NK, at=0)
        cut = parts("MIX_RINGS", 2 * BATCH * D_MODEL)
        RING_U = cut(BATCH, D_MODEL)
        RING_V = cut(BATCH, D_MODEL)
        XA = cut(RC, XA_W, at=0)
        XC = cut(RC, XC_W)
        RG = cut(RC, XC_W)
        IG = cut(RC, XC_W)
        DEC = cut(RC, XC_W)
        XQ = cut(RC, XQ_W)
        S1 = cut(RC, XQ_W)
        S2 = cut(RC, XQ_W)
        OALL = cut(TILES, HEADS, HW)
        ZH = cut(2, TILES * 3 * HW)
        ZH = [ZH[:, i, :].rearrange("p (t n) -> p t n", t=TILES) for i in range(2)]
        SUMS = [(S1, S2)[c % 2][:, c, :] for c in range(RC)]
        POOL_PARTS = ((POOL_HIST, SEQ, 0), (XQ_S + POOL_HIST, DEC_SEQ, SEQ))
        MT = cut(KC, TOKD, at=0)
        cut(TILES * HEADS * HW)
        SG = cut(2, N_BRANCH, TOK)
        MTMP = cut(TOK)
        QT = cut(2, TOKD, at=0)
        KT = cut(2 * PAST + P)
        PR = [cut(2, P), cut(2, 2 * P), cut(2, PAST + DEC_SEQ)]
        PC = [cut(P), cut(2 * P), cut(3 * P)]
        PTA = cut(3 * P)
        PTB = cut(3 * P)
        SQ = cut(TILES, HW)
        rows = cut(D_RNN, at=10672)
        SKR = cut(2, NK)
        LAMV = cut(4, HD)
        POOLW = cut(RC, P)

        PT = sb("PT", [P, RC, NROW])
        nsp = sb("nsp", [P, RC])
        spt = sb("spt", [P, 3, RC])
        SKT = sb("SKT", [P, 2, NK])
        BDA = sb("BDA", [P, RC, P])
        BDX = sb("BDX", [P, RC, P])
        SO = sb("SO", [P, RC, P])
        SOT = sb("SOT", [P, D_RNN])
        LD = sb("LD", [P, 2])
        LE = sb("LE", [P, 2])
        neg_lam = sb("neg_lam", [P, 1])
        LCON = sb("LCON", [P, 3])
        SUBG = sb("SUBG", [P, 1])
        QS = sb("QS", [P, 2, TOKD])
        ident = sb("ident", [P, P])
        twins = sb("twins", [P, P])
        eps_c = sb("eps_c", [P, 1])
        iota16 = sb("iota16", [P, TOPK])
        ROTT = sb("ROTT", [P, TILES, 2, ROT])
        PINV = sb("PINV", [P, 4, TOK])
        ss = sb("ss", [P, TILES])
        sd = sb("sd", [P, TILES])
        rstd = sb("rstd", [P, TILES])
        sso = sb("sso", [P, TILES, HEADS])
        rso = sb("rso", [P, TILES, HEADS])

        CKV = sb("CKV", [P, 2, 2, 2, HW])
        CK = [CKV[:, i, 0] for i in range(2)]
        CV = [CKV[:, i, 1] for i in range(2)]
        HOT = sb("HOT", [P, 2, TOPK * TOPK])
        rot_a = sb("rot_a", [P, 4, TILES, 4, ROT])
        mxs = sb("mxs", [P, TILES, 2])
        nb = sb("nb", [P, TILES, 2])
        sme = sb("sme", [P, TILES, 2])
        rec = sb("rec", [P, TILES, 2])
        MX = sb("MX", [P, 2, TOPK])
        IX = sb("IX", [P, 2, TOPK], U32)
        IXF = sb("IXF", [P, 2, TOPK])
        BS = sb("BS", [P, TOPK])
        BC = sb("BC", [P, TOPK], U32)
        CI = sb("CI", [P, 2, TOPK], U32)
        CIF = sb("CIF", [P, 2, TOPK])
        I12 = sb("I12", [P, 2, TOPK])
        IDF = sb("IDF", [P, TOPK])
        IDX = sb("IDX", [P, TOPK], U32)
        STI = sb("STI", [P, 3, BATCH], U32)
        BSM = sb("BSM", [P, TOPK])
        GEX = sb("GEX", [P, TOPK])
        GSM = sb("GSM", [P, 1])
        GRC = sb("GRC", [P, 1])
        GATE = sb("GATE", [P, TOPK])
        AV = sb("AV", [P, BATCH])
        GV = sb("GV", [P, BATCH])
        WV = sb("WV", [P, BATCH])

        ps = ctx.enter_context(nc.psum_tensor("ps", [P, 8 * 512], F32))

        def bank(i, a=0, b=512):
            return ps[:, i * 512 + a:i * 512 + b]

        setup = signal("setup", 0)
        loaded_x = landing("loaded_x", 0)
        loaded_t = landing("loaded_t", 0)
        gain_in = landing("gain_in", 2)
        gain_used = signal("gain_used", 1)
        w_in_slot = [landing(f"w_in_slot{i}", SLOT_USES[i]) for i in range(SLOTS)]
        w_used = [signal(f"w_used{i}", SLOT_USES[i], start=1) for i in range(SLOTS)]
        qkv_in = [landing(f"qkv_in{i}", 3 * HEADS // 2) for i in range(2)]
        qkv_used = [signal(f"qkv_used{i}", HEADS // 2, start=1) for i in range(2)]
        cache_in = [landing(f"cache_in{i}", 2 * HEADS // 2) for i in range(2)]
        layer_done = signal("layer_done", 4, start=1)
        par_ps = signal("par_ps", 2)
        par_sb = signal("par_sb", 2)
        lam_dot = signal("lam_dot", 1)
        lam_exp = signal("lam_exp", 1)
        sp_in = signal("sp_in", 1)
        sp_ln = signal("sp_ln", 1)
        sp_out = signal("sp_out", 1)
        sq_done = signal("sq_done", 2 * TILES)
        hn_ready = signal("hn_ready", 2 * TILES)
        nt_ps = signal("nt_ps", 2 * TILES * TURNS)
        nt_ev = signal("nt_ev", 2 * TILES * TURNS)
        ff_ps = signal("ff_ps", 12)
        ff_ev = signal("ff_ev", 12)
        xc_ready = signal("xc_ready", 1)
        bd_ps = signal("bd_ps", 2 * RC)
        sig_ev = signal("sig_ev", 2 * RC)
        decay = signal("decay", 1)
        oma = signal("oma", 1)
        root = signal("root", 1)
        ya_ready = signal("ya_ready", 1)
        d_ready = signal("d_ready", 1)
        pl_ps = signal("pl_ps", RC)
        pl_ev = signal("pl_ev", RC)
        so_ready = signal("so_ready", 1)
        so_ps = signal("so_ps", 1)
        so_sb = signal("so_sb", 1)
        so_out = landing("so_out", 6)
        z_ps = signal("z_ps", TILES * HEADS)
        z_ev = signal("z_ev", TILES * HEADS)
        rot_mul = signal("rot_mul", 4 * HEADS)
        rot_done = signal("rot_done", 2 * HEADS, start=1)
        kv_out = [landing(f"kv_out{i}", 4 * HEADS // 2) for i in range(2)]
        kv_stored = signal("kv_stored", HEADS, start=1)
        qt_ps = signal("qt_ps", HEADS)
        qt_ev = signal("qt_ev", 2 * HEADS)
        kt_ps = signal("kt_ps", HEADS)
        kt_ev = signal("kt_ev", HEADS)
        s_ps = signal("s_ps", TILES * HEADS)
        nb_ready = signal("nb_ready", TILES * HEADS)
        ex_done = signal("ex_done", 2 * TILES * HEADS, start=1)
        p_ready = signal("p_ready", TILES * HEADS)
        pta_ps = signal("pta_ps", HEADS)
        ptb_ps = signal("ptb_ps", HEADS)
        pta_ev = signal("pta_ev", HEADS, start=1)
        ptb_ev = signal("ptb_ev", HEADS, start=1)
        att_done = signal("att_done", HEADS, start=1)
        cache_free = signal("cache_free", HEADS, start=2)
        o_ev = signal("o_ev", HEADS, start=1)
        sso_ready = signal("sso_ready", 1)
        sso_root = signal("sso_root", 1)
        on_ready = signal("on_ready", 1)
        yt_ps = signal("yt_ps", HEADS)
        yt_ev = signal("yt_ev", HEADS)
        projab_in = landing("projab_in", GB)
        gate_ps = signal("gate_ps", N_BRANCH * KC)
        sg_ev = signal("sg_ev", N_BRANCH * KC, start=N_BRANCH)
        proj_ps = signal("proj_ps", KC)
        m_ev = signal("m_ev", KC, start=2)
        mt_ready = signal("mt_ready", 1)
        x_done = signal("x_done", 2)
        xo_ps = signal("xo_ps", GB * TILES)
        xo_ev = signal("xo_ev", GB * TILES)
        pq_ps = signal("pq_ps", Q_BLOCKS)
        pq_ev = signal("pq_ev", Q_BLOCKS, start=2)
        sc_ps = signal("sc_ps", Q_BLOCKS)
        sc_ev = signal("sc_ev", Q_BLOCKS, start=2)
        best_ready = signal("best_ready", TILES * PH)
        gex_ready = signal("gex_ready", TILES * PH)
        idx_staged = signal("idx_staged", BATCHES)
        u_in = [landing(f"u_in{i}", BATCHES) for i in range(BATCH)]
        v_in = [landing(f"v_in{i}", BATCHES) for i in range(BATCH)]
        u_free = signal("u_free", BATCHES * BATCH, start=BATCH)
        v_free = signal("v_free", BATCHES * BATCH, start=BATCH)
        av_ready = signal("av_ready", BATCHES)
        gv_ready = signal("gv_ready", BATCHES)
        wv_ready = signal("wv_ready", BATCHES)
        dg_ready = signal("dg_ready", BATCHES * BATCH)
        acc_clear = signal("acc_clear", TILES)
        y_ready = signal("y_ready", 0)
        stored = landing("stored", 0)

        def xo_bank(n):
            return 6 + n % 2 if n < 2 * GB else n - 2 * GB

        def bcast(row):
            return row.partition_broadcast(P)

        def small_loads(l):
            def row(name, n=1):
                return rows[ROW[name]:ROW[name] + n, :]

            def diag(t, half):
                a = half * HD
                return t[a:a + HD, :, a:a + HD]

            def blocks(w, half):
                return w[l].rearrange("(c two) i j -> two i c j", two=2)[half]

            return [
                (row("conv_state", CONV_HIST), state_conv[l, 0]),
                (row("pool_state", POOL_HIST), state_pool[l, 0]),
                (row("lru_state"), state_lru[l]),
                (row("conv_w", CONV_W), conv_w[l]),
                (row("conv_b"), conv_b[bass.ds(l, 1)]),
                (row("lru_ba"), lru_ba[bass.ds(l, 1)]),
                (row("lru_bx"), lru_bx[bass.ds(l, 1)]),
                (row("lru_L"), lru_L[bass.ds(l, 1)]),
                (row("pool_scale"), pool_scale[bass.ds(l, 1)]),
                (SKR[:, :, :], peer_subkeys[l].rearrange("a k d -> k a d")),
                (POOLW[:, :, :], pool_w[l].rearrange("g c d -> c g d")),
                (diag(BDA, 0), blocks(lru_wa, 0)),
                (diag(BDA, 1), blocks(lru_wa, 1)),
                (diag(BDX, 0), blocks(lru_wx, 0)),
                (diag(BDX, 1), blocks(lru_wx, 1)),
                (LAMV[:, 0, :], bcast(lam_q1[l])),
                (LAMV[:, 1, :], bcast(lam_k1[l])),
                (LAMV[:, 2, :], bcast(lam_q2[l])),
                (LAMV[:, 3, :], bcast(lam_k2[l])),
                (LCON[:, :], bcast(layer_consts[l])),
                (SUBG[:, :], subln_g[bass.ds(l, 1)].rearrange("a e -> e a")),
            ]

        NSMALL = 21
        small_in = landing("small_in", NSMALL)
        block = ctx.enter_context(nc.Block())

        @block.sync
        def _(sp):
            for t in range(2):
                sp.dma_start(X[:, t, :], x_prompt[0, t * P:(t + 1) * P, :]).then_inc(loaded_x.sem, 16)
            sp.dma_start(X[0:CHUNK, 2, :], x_sample[0]).then_inc(loaded_x.sem, 16)
            sp.dma_start(X[CHUNK:P, 2, :], x_sample[0]).then_inc(loaded_x.sem, 16)
            sp.wait_ge(setup.sem, 8)

            def unit(l, slot, n, srcs):
                sp.wait_ge(*w_used[slot].at(l, n))
                at = 0
                for k, src in enumerate(srcs):
                    c = src.shape[0] // P
                    i = sp.dma_start(W[:, slot, at:at + c, :], src.rearrange("(c p) n -> p c n", p=P))
                    at += c
                    i.then_inc(w_in_slot[slot].sem, 16)

            with sp.Fori(0, DEPTH) as l:
                def ff_unit(u):
                    kind, j = FF_UNITS[u]
                    unit(l, u % SLOTS, u // SLOTS,
                         [w_in[l, :, kind * D_RNN + j * UNIT:kind * D_RNN + (j + 1) * UNIT]])

                ff_unit(0)
                sp.wait_ge(*layer_done.at(l, 0))
                sp.dma_start(G[:, :], bcast(norm1_g[l])).then_inc(gain_in.sem, 16)
                ff_unit(1)
                loads = small_loads(l)
                assert len(loads) == NSMALL
                for dst, src in loads:
                    sp.dma_start(dst, src).then_inc(small_in.sem, 16)
                for u in range(2, 3 * HB):
                    ff_unit(u)

                with sp.Fori(0, HEADS // 2) as g:
                    for par in range(2):
                        h = g * 2 + par
                        sp.wait_ge(*qkv_used[par].at(l, g))
                        for part in range(3):
                            col = COL_Q + part * HEADS * HW + h * HW
                            sp.dma_start(
                                WQKV[par][:, :, part * HW:(part + 1) * HW],
                                w_in[l, :, bass.ds(col, HW)].rearrange("(c p) n -> p c n", p=P))\
                                .then_inc(qkv_in[par].sem, 16)
                        sp.wait_ge(*cache_free.at(l, h - 1))
                        sp.dma_start(CK[par], cache_k[l, 0, :, h].rearrange("(t p) m d -> p t (m d)", p=P))\
                            .then_inc(cache_in[par].sem, 16)
                        sp.dma_start(CV[par], cache_v[l, 0, :, h].rearrange("(t p) e -> p t e", p=P))\
                            .then_inc(cache_in[par].sem, 16)

                sp.wait_ge(*gain_used.at(l, 1))
                sp.dma_start(G[:, :], bcast(norm2_g[l])).then_inc(gain_in.sem, 16)
                with sp.Fori(0, GB) as i:
                    for b in range(N_BRANCH):
                        sp.wait_ge(*w_used[b].at(l, i + (2 if b == 0 else 1)))
                        sp.dma_start(W[:, b, :, :],
                                     w_in[l, :, bass.ds(COL_G + b * D_MODEL + i * UNIT, UNIT)]
                                     .rearrange("(c p) n -> p c n", p=P)).then_inc(w_in_slot[b].sem, 16)
                    sp.wait_ge(*w_used[3].at(l, i + 1))
                    sp.dma_start(W[:, 3, 0:RC, :], proj_a[l, :, bass.ds(i * UNIT, UNIT)]
                                 .rearrange("(c p) n -> p c n", p=P)).then_inc(projab_in.sem, 16)
                    sp.dma_start(W[:, 3, RC:2 * RC, :], proj_b[l, :, bass.ds(i * UNIT, UNIT)]
                                 .rearrange("(c p) n -> p c n", p=P)).then_inc(w_in_slot[3].sem, 16)
                    sp.wait_ge(*w_used[4].at(l, i + 1))
                    sp.dma_start(W[:, 4, :, :], proj_c[l, :, bass.ds(i * UNIT, UNIT)]
                                 .rearrange("(c p) n -> p c n", p=P)).then_inc(w_in_slot[4].sem, 16)
                for u in range(GB):
                    unit(l, u, GB + (2 if u == 0 else 1), [w_out[l, :, u * UNIT:(u + 1) * UNIT]])

                def q_unit(slot, use, u):
                    sp.wait_ge(*w_used[slot].at(l, use))
                    sp.nop(nofuse=True)
                    sp.dma_start(W[:, slot, :, :], peer_wq[l, :, bass.ds(u * UNIT, UNIT)]
                                 .rearrange("(c p) n -> p c n", p=P)).then_inc(w_in_slot[slot].sem, 16)

                for u, slot in enumerate(FIRST_Q):
                    q_unit(slot, BEFORE_Q[slot], u)
                with sp.Fori(0, PH - 2) as h:
                    q_unit(NEXT_Q, h + BEFORE_Q[NEXT_Q], h + 2)
            sp.wait_ge(*layer_done.at(DEPTH, 0))
            sp.dma_start(G[:, :], bcast(final_g)).then_inc(gain_in.sem, 16)
            sp.wait_ge(y_ready.sem, 1)
            sp.dma_start(y_prompt[0].rearrange("(t p) d -> p t d", p=P), HN[:, 0:2, :]).then_inc(stored.sem, 16)
            sp.dma_start(y_sample[0], HN[0:DEC_SEQ, 2, :]).then_inc(stored.sem, 16)
            sp.wait_ge(stored.sem, 32)

        @block.gpsimd
        def _(pool):
            for s in started:
                pool.sem_inc(s.sem, s.start)
            pool.memset(ident[:, :], 0.0).then_inc(setup.sem, 1)
            pool.memset(twins[:, :], 0.0).then_inc(setup.sem, 1)
            pool.memset(rows[:, :], 0.0).then_inc(setup.sem, 1)
            pool.memset(BDA[:, :, :], 0.0).then_inc(setup.sem, 1)
            pool.memset(BDX[:, :, :], 0.0).then_inc(setup.sem, 1)
            pool.memset(SO[:, :, :], 0.0).then_inc(setup.sem, 1)
            pool.memset(eps_c[:, :], EPS).then_inc(setup.sem, 1)
            pool.memset(iota16[:, :], 0.0).then_inc(setup.sem, 1)
            pool.wait_ge(setup.sem, 8)
            pool.affine_select(out=ident[:, :], in_=ident[:, :], compare_op=ALU.not_equal, fill=1.0,
                               base=0, pattern=[[-1, P]], channel_multiplier=1).then_inc(setup.sem, 1)
            pool.iota(iota16[:, :], [[1, TOPK]], base=0, channel_multiplier=0,
                      allow_small_or_imprecise_dtypes=True).then_inc(setup.sem, 1)
            for n, base in enumerate((0, CHUNK, -CHUNK)):
                pool.affine_select(out=twins[:, :], in_=twins[:, :], compare_op=ALU.not_equal, fill=1.0,
                                   base=base, pattern=[[-1, P]], channel_multiplier=1).then_inc(setup.sem, 1)
                pool.wait_ge(setup.sem, 11 + n)
            pool.dma_start(ROTT[:, :, :, :], rot_table.rearrange("t p a r -> p t a r"))\
                .then_inc(loaded_t.sem, 16)
            pool.dma_start(PINV[:, :, :], pool_inv.partition_broadcast(P)).then_inc(loaded_t.sem, 16)
            pool.wait_ge(loaded_t.sem, 2 * 16)

            def rotary(l, h_before, par):
                h = h_before * 2 + par
                z = ZH[par][:, :, 0:2 * HW].rearrange("p t (m d) -> p t m d", m=4)
                x1, x2 = z[:, :, :, 0:ROT], z[:, :, :, ROT:2 * ROT]
                cos = ROTT[:, :, 0, :].unsqueeze(2).to_broadcast([P, TILES, 4, ROT])
                sin = ROTT[:, :, 1, :].unsqueeze(2).to_broadcast([P, TILES, 4, ROT])
                pool.wait_ge(*z_ev.at(l, h * TILES + TILES))
                pool.wait_ge(*rot_done.at(l, h * 2))
                for n, (a, b) in enumerate(((x1, cos), (x2, sin), (x2, cos), (x1, sin))):
                    pool.tensor_tensor(rot_a[:, n], a, b, ALU.mult).then_inc(rot_mul.sem, 1)
                pool.wait_ge(*rot_mul.at(l, h * 4 + 4))
                pool.tensor_tensor(x1, rot_a[:, 0], rot_a[:, 1], ALU.subtract).then_inc(rot_done.sem, 1)
                pool.tensor_tensor(x2, rot_a[:, 2], rot_a[:, 3], ALU.add).then_inc(rot_done.sem, 1)
                pool.wait_ge(*rot_done.at(l, h * 2 + 2))
                kcol, vcol = slice(HW, 2 * HW), slice(2 * HW, 3 * HW)
                pool.dma_start(k_prompt[l, 0, :, h].rearrange("(t p) m d -> p t (m d)", p=P),
                               ZH[par][:, 0:2, kcol]).then_inc(kv_out[par].sem, 16)
                pool.dma_start(v_prompt[l, 0, :, h].rearrange("(t p) e -> p t e", p=P),
                               ZH[par][:, 0:2, vcol]).then_inc(kv_out[par].sem, 16)
                pool.dma_start(k_sample[l, 0, :, h].rearrange("p m d -> p (m d)"),
                               ZH[par][0:DEC_SEQ, 2, kcol]).then_inc(kv_out[par].sem, 16)
                pool.dma_start(v_sample[l, 0, :, h], ZH[par][0:DEC_SEQ, 2, vcol]).then_inc(kv_out[par].sem, 16)
                pool.wait_ge(*kv_out[par].at(l, h_before * 4 + 4))
                pool.sem_inc(kv_stored.sem, 1)

            table_u = peer_u.rearrange("l e d -> (l e) d")
            table_v = peer_v.rearrange("l e d -> (l e) d")

            def gathers(l, b, i):
                pool.wait_ge(*idx_staged.at(l, b + 1))
                for s in range(BATCH):
                    pool.wait_ge(*u_free.at(l, b * BATCH + (s + 1 - BATCH)))
                    pool.nop(nofuse=True)
                    pool.indirect_dma_start(RING_U[:, s, :], None, table_u,
                                            bass.IndirectOffsetOnAxis(STI[:, i, s:s + 1], 0))\
                        .then_inc(u_in[s].sem, 16)
                for s in range(BATCH):
                    pool.wait_ge(*v_free.at(l, b * BATCH + (s + 1 - BATCH)))
                    pool.nop(nofuse=True)
                    pool.indirect_dma_start(RING_V[:, s, :], None, table_v,
                                            bass.IndirectOffsetOnAxis(STI[:, i, s:s + 1], 0))\
                        .then_inc(v_in[s].sem, 16)

            with pool.Fori(0, DEPTH) as l:
                with pool.Fori(0, HEADS // 2) as g:
                    for par in range(2):
                        rotary(l, g, par)
                pool.wait_ge(*so_sb.at(l, 1))
                for dst, at, n in ((conv_prompt[l, 0], ST_CP, CONV_HIST), (pool_prompt[l, 0], ST_PP, POOL_HIST),
                                   (conv_sample[l, 0], ST_CS, CONV_HIST), (pool_sample[l, 0], ST_PS, POOL_HIST),
                                   (lru_prompt[l], ST_LP, 1), (lru_sample[l], ST_LS, 1)):
                    pool.dma_start(dst, SOT[at:at + n, :]).then_inc(so_out.sem, 16)
                with pool.Fori(0, PH) as h:
                    for i in range(2):
                        gathers(l, h * 2 + i, i)
                with pool.Fori(0, PH) as h:
                    for i in range(3):
                        gathers(l, h * 3 + (FIRST_B + i), i)
                pool.wait_ge(*so_out.at(l, 6))
                pool.nop(nofuse=True)
                pool.drain().then_inc(layer_done.sem, 1)
                pool.wait_ge(*layer_done.at(l, 4))

        @block.tensor
        def _(pe):
            pe.wait_ge(setup.sem, 13)

            def norm_turn(l, n, tiles):
                for t in tiles:
                    pe.wait_ge(*hn_ready.at(l, n * TILES + t + 1))
                    for a in range(TURNS):
                        done = (n * TILES + t) * TURNS + a
                        if done >= 2:
                            pe.wait_ge(*nt_ev.at(l, done - 1))
                        for c in range(KC // TURNS):
                            i = pe.transpose(bank(2 + a, c * P, (c + 1) * P),
                                             HN[:, t, (a * KC // TURNS + c) * P:(a * KC // TURNS + c + 1) * P],
                                             ident[:, :])
                        i.then_inc(nt_ps.sem, 1)

            def qkv(l, h, par, tiles):
                for t in tiles:
                    if t == 0:
                        pe.wait_ge(*qkv_in[par].at(l, (h - par) // 2 * 3 + 3) if isinstance(h, int)
                                   else (qkv_in[par].sem, (l * (3 * HEADS // 2) + (h[0] * 3 + 3)) * 16))
                    n = None
                    hh = h if isinstance(h, int) else h[0] * 2 + h[1]
                    b = (par * TILES + t) % 2
                    if not (isinstance(h, int) and h == 0 and t < 2):
                        pe.wait_ge(*z_ev.at(l, hh * TILES + (t - 1)))
                    for c in range(KC):
                        i = pe.matmul(bank(b, 0, 3 * HW), HT[:, c, t * P:(t + 1) * P], WQKV[par][:, c, :],
                                      start=c == 0, stop=c == KC - 1)
                    i.then_inc(z_ps.sem, 1)
                    if t == TILES - 1:
                        pe.drain().then_inc(qkv_used[par].sem, 1)

            def gate(l, g, k, b):
                dc = g * 2 + k
                pe.wait_ge(*sg_ev.at(l, dc * N_BRANCH + (b + 1 - N_BRANCH)))
                if k == 0:
                    pe.wait_ge(*w_in_slot[b].at(l, g + FF_USES[b] + 1))
                for c in range(KC):
                    i = pe.matmul(bank(b, 0, TOK), W[:, b, c, k * P:(k + 1) * P], HT[:, c, 0:TOK],
                                  start=c == 0, stop=c == KC - 1)
                i.then_inc(gate_ps.sem, 1)
                if k == 1:
                    pe.drain().then_inc(w_used[b].sem, 1)

            def branches(l, g, k):
                dc = g * 2 + k
                cols = slice(k * P, (k + 1) * P)
                pe.wait_ge(*m_ev.at(l, dc))
                if k == 0:
                    pe.wait_ge(*w_in_slot[3].at(l, g + FF_USES[3] + 1))
                    pe.wait_ge(*projab_in.at(l, g + 1))
                for c in range(RC):
                    pe.matmul(bank(3, 0, TOK), W[:, 3, c, cols], YT[:, c, :],
                              start=c == 0, stop=c == RC - 1)
                for c in range(RC):
                    i = pe.matmul(bank(4, 0, TOK), W[:, 3, RC + c, cols], YT[:, RC + c, :],
                                  start=c == 0, stop=c == RC - 1)
                if k == 1:
                    i.then_inc(w_used[3].sem, 1)
                if k == 0:
                    pe.wait_ge(*w_in_slot[4].at(l, g + FF_USES[4] + 1))
                for c in range(HEADS):
                    i = pe.matmul(bank(5, 0, TOK), W[:, 4, c, cols], YT[:, 2 * RC + c, :],
                                  start=c == 0, stop=c == HEADS - 1)
                i.then_inc(proj_ps.sem, 1)
                if k == 1:
                    pe.drain().then_inc(w_used[4].sem, 1)

            def head(l, g, par, nxt):
                h = g * 2 + par
                z = ZH[par]
                pe.wait_ge(*rot_done.at(l, h * 2 + 2))
                pe.wait_ge(*ex_done.at(l, h * 2 * TILES))
                for t in range(TILES):
                    i = pe.transpose(bank(2, t * P, (t + 1) * P), z[:, t, 0:HW], ident[:, :])
                i.then_inc(qt_ps.sem, 1)
                pe.wait_ge(*pta_ev.at(l, h))
                for t in range(TILES):
                    pe.transpose(bank(3, t * P, (t + 1) * P), z[:, t, HW:2 * HW], ident[:, :])
                pe.wait_ge(cache_in[par].sem, (l * HEADS + (g * 2 + 2)) * 16)
                for t in range(2):
                    i = pe.transpose(bank(5, t * P, (t + 1) * P), CK[par][:, t, :], ident[:, :])
                i.then_inc(kt_ps.sem, 1)
                if nxt:
                    qkv(l, nxt, 1 - par, [0])
                pe.wait_ge(*qt_ev.at(l, h * 2 + 2))
                pe.wait_ge(*kt_ev.at(l, h + 1))
                pe.wait_ge(*ptb_ev.at(l, h))
                for t in range(2):
                    n = (t + 1) * P
                    for m in range(2):
                        out = bank(4 if t == 0 else 6, m * n, (m + 1) * n)
                        i = pe.matmul(out, QT[:, m, t * P:(t + 1) * P], KT[:, 0:n], start=True, stop=True)
                    i.then_inc(s_ps.sem, 1)
                for m in range(2):
                    i = pe.matmul(bank(5 if m == 0 else 2, 0, PAST + DEC_SEQ), QT[:, m, 2 * P:3 * P],
                                  KT[:, SEQ:SEQ + PAST + DEC_SEQ], start=True, stop=True)
                i.then_inc(s_ps.sem, 1)
                if nxt:
                    qkv(l, nxt, 1 - par, [1, 2])
                else:
                    gate(l, 0, 0, 0)
                for t in range(2):
                    pe.wait_ge(*p_ready.at(l, h * TILES + t + 1))
                    for c in range(t + 1):
                        i = pe.transpose(bank(3, (t + c) * P, (t + c + 1) * P), PC[t][:, c * P:(c + 1) * P],
                                         ident[:, :])
                i.then_inc(pta_ps.sem, 1)
                pe.wait_ge(*p_ready.at(l, h * TILES + 3))
                for c in range(3):
                    i = pe.transpose(bank(4, c * P, (c + 1) * P), PC[2][:, c * P:(c + 1) * P], ident[:, :])
                i.then_inc(ptb_ps.sem, 1)
                pe.wait_ge(*o_ev.at(l, h))
                pe.wait_ge(*pta_ev.at(l, h + 1))
                v = [z[:, t, 2 * HW:3 * HW] for t in range(TILES)]
                pe.matmul(bank(7, 0, P), PTA[:, 0:P], v[0], start=True, stop=True)
                pe.matmul(bank(7, P, 2 * P), PTA[:, P:2 * P], v[0], start=True, stop=False)
                pe.matmul(bank(7, P, 2 * P), PTA[:, 2 * P:3 * P], v[1], start=False, stop=True)
                pe.wait_ge(*ptb_ev.at(l, h + 1))
                for c, vv in enumerate((CV[par][:, 0, :], CV[par][:, 1, :], v[2])):
                    i = pe.matmul(bank(7, 2 * P, 3 * P), PTB[:, c * P:(c + 1) * P], vv,
                                  start=c == 0, stop=c == 2)
                i.then_inc(att_done.sem, 1)
                pe.drain().then_inc(cache_free.sem, 1)

            def experts(l, b, t):
                for s in range(BATCH):
                    pe.wait_ge(*dg_ready.at(l, b * BATCH + s + 1))
                    pe.wait_ge(*v_in[s].at(l, b + 1))
                    for j in range(2):
                        i = pe.matmul(bank(2 * t + j), DG[:, s, :], RING_V[:, s, j * 512:(j + 1) * 512],
                                      start=False, stop=False, skip_group_check=True)
                    i.then_inc(v_free.sem, 1)

            with pe.Fori(0, DEPTH) as l:
                norm_turn(l, 0, range(TILES))
                pe.wait_ge(*nt_ev.at(l, TILES * TURNS))

                def ff(u):
                    pe.wait_ge(*w_in_slot[u % SLOTS].at(l, u // SLOTS + 1))
                    for k in range(2):
                        n = 2 * u + k
                        if n >= 2:
                            pe.wait_ge(*ff_ev.at(l, n - 1))
                        for c in range(KC):
                            i = pe.matmul(bank(4 + n % 2, 0, TOK), W[:, u % SLOTS, c, k * P:(k + 1) * P],
                                          HT[:, c, 0:TOK], start=c == 0, stop=c == KC - 1)
                        i.then_inc(ff_ps.sem, 1)
                    pe.drain().then_inc(w_used[u % SLOTS].sem, 1)

                ff(0)
                pe.wait_ge(*small_in.at(l, NSMALL))
                for c in range(RC):
                    i = pe.transpose(bank(0, c * P, (c + 1) * P), rows[:, c * P:(c + 1) * P], ident[:, :])
                i.then_inc(par_ps.sem, 1)
                for a in range(2):
                    i = pe.transpose(bank(1, a * P, (a + 1) * P), SKR[:, a, :], ident[:, :])
                i.then_inc(par_ps.sem, 1)
                for u in range(1, 5):
                    ff(u)
                pe.wait_ge(*xc_ready.at(l, 1))
                for c in range(RC):
                    for j, wt in enumerate((BDA, BDX)):
                        if c >= 1:
                            pe.wait_ge(*sig_ev.at(l, 2 * c - 1 + j))
                        pe.matmul(bank(6 + j, 0, XC_W), wt[:, c, :], XC[:, c, :],
                                  start=True, stop=True).then_inc(bd_ps.sem, 1)
                ff(5)
                pe.wait_ge(*par_sb.at(l, 2))
                qkv(l, 0, 0, range(TILES))
                pe.wait_ge(*d_ready.at(l, 1))
                pe.wait_ge(*ff_ev.at(l, 12))
                for c in range(RC):
                    if c >= 2:
                        pe.wait_ge(*pl_ev.at(l, c - 1))
                    for a, n, at in POOL_PARTS:
                        i = pe.matmul(bank(4 + c % 2, at, at + n), POOLW[:, c, :], SUMS[c][:, a:a + n],
                                      start=True, stop=True)
                    i.then_inc(pl_ps.sem, 1)
                pe.wait_ge(*so_ready.at(l, 1))
                pe.wait_ge(*sig_ev.at(l, 2 * RC))
                for c in range(RC):
                    i = pe.transpose(bank(6, c * P, (c + 1) * P), SO[:, c, :], ident[:, :])
                i.then_inc(so_ps.sem, 1)
                pe.wait_ge(*pl_ev.at(l, RC))
                pe.wait_ge(*so_sb.at(l, 1))
                pe.nop(nofuse=True)
                with pe.Fori(0, HEADS // 2 - 1) as g:
                    head(l, g, 0, (g, 1))
                    head(l, g, 1, (g + 1, 0))
                head(l, HEADS // 2 - 1, 0, (HEADS // 2 - 1, 1))
                head(l, HEADS // 2 - 1, 1, None)
                gate(l, 0, 0, 1)
                gate(l, 0, 0, 2)
                pe.wait_ge(*on_ready.at(l, 1))
                for hh in range(HEADS):
                    if hh >= 2:
                        pe.wait_ge(*yt_ev.at(l, hh - 1))
                    for t in range(TILES):
                        i = pe.transpose(bank(6 + hh % 2, t * P, (t + 1) * P), OALL[:, t, hh, :], ident[:, :])
                    i.then_inc(yt_ps.sem, 1)
                pe.wait_ge(*yt_ev.at(l, HEADS))
                pe.nop(nofuse=True)
                def merge(g, last):
                    for b in range(N_BRANCH):
                        gate(l, g, 1, b)
                    branches(l, g, 0)
                    if not last:
                        for b in range(N_BRANCH):
                            gate(l, g + 1, 0, b)
                    branches(l, g, 1)

                with pe.Fori(0, GB - 1) as g:
                    merge(g, False)
                merge(GB - 1, True)
                def output(t):
                    for u in range(GB):
                        n = t * GB + u
                        if t == 0:
                            pe.wait_ge(*w_in_slot[u].at(l, BEFORE_Q[u]))
                        if 2 <= n < 2 * GB:
                            pe.wait_ge(*xo_ev.at(l, n - 1))
                        for c in range(KC):
                            i = pe.matmul(bank(xo_bank(n), 0, UNIT), MT[:, c, t * P:(t + 1) * P], W[:, u, c, :],
                                          start=c == 0, stop=c == KC - 1)
                        i.then_inc(xo_ps.sem, 1)
                        if t == TILES - 1:
                            pe.drain().then_inc(w_used[u].sem, 1)

                def queries(n, k, slot, tiles, free):
                    a, b = tiles[0] * P, (tiles[-1] + 1) * P
                    pe.wait_ge(*pq_ev.at(l, n + (k - 1)))
                    for c in range(KC):
                        i = pe.matmul(bank(4 + k, 0, b - a), W[:, slot, c, k * P:(k + 1) * P], HT[:, c, a:b],
                                      start=c == 0, stop=c == KC - 1)
                    i.then_inc(pq_ps.sem, 1)
                    if free:
                        pe.drain().then_inc(w_used[slot].sem, 1)

                def key_scores(n, tiles):
                    for k in range(2):
                        pe.wait_ge(*pq_ev.at(l, n + (k + 1)))
                        pe.wait_ge(*sc_ev.at(l, n + (k - 1)))
                        for t in range(len(tiles)):
                            i = pe.matmul(bank(6 + k, t * P, (t + 1) * P), QS[:, k, t * P:(t + 1) * P],
                                          SKT[:, k, :], start=True, stop=True)
                        i.then_inc(sc_ps.sem, 1)

                pe.wait_ge(*mt_ready.at(l, 1))
                output(0)
                output(1)
                norm_turn(l, 1, [0])
                pe.wait_ge(*nt_ev.at(l, (TILES + 1) * TURNS))
                pe.wait_ge(*xo_ev.at(l, 2 * GB))
                pe.wait_ge(*w_in_slot[FIRST_Q[0]].at(l, BEFORE_Q[FIRST_Q[0]] + 1))
                for k in range(2):
                    queries(0, k, FIRST_Q[0], [0], False)
                key_scores(0, [0])
                output(2)
                pe.wait_ge(*xo_ev.at(l, GB * TILES))
                norm_turn(l, 1, [1, 2])
                pe.wait_ge(*nt_ev.at(l, 2 * TILES * TURNS))
                for k in range(2):
                    queries(2, k, FIRST_Q[0], [1, 2], k == 1)
                key_scores(2, [1, 2])
                pe.wait_ge(*w_in_slot[FIRST_Q[1]].at(l, BEFORE_Q[FIRST_Q[1]] + 1))
                for k in range(2):
                    queries(4, k, FIRST_Q[1], range(TILES), k == 1)
                key_scores(4, range(TILES))
                pe.wait_ge(*acc_clear.at(l, 1))
                pe.nop(nofuse=True)
                with pe.Fori(0, PH - 2) as h:
                    n = h * 2 + 6
                    experts(l, h * 2, 0)
                    pe.wait_ge(*w_in_slot[NEXT_Q].at(l, h + (BEFORE_Q[NEXT_Q] + 1)))
                    queries(n, 0, NEXT_Q, range(TILES), False)
                    experts(l, h * 2 + 1, 0)
                    queries(n, 1, NEXT_Q, range(TILES), True)
                    key_scores(n, range(TILES))
                with pe.Fori(FIRST_B - 4, FIRST_B) as b:
                    experts(l, b, 0)
                pe.wait_ge(*acc_clear.at(l, 3))
                pe.nop(nofuse=True)
                with pe.Fori(0, PH) as h:
                    for i, t in enumerate((1, 1, 2)):
                        experts(l, h * 3 + (FIRST_B + i), t)
                pe.drain().then_inc(layer_done.sem, 1)
                pe.wait_ge(*layer_done.at(l, 4))

        @block.scalar
        def _(act):
            act.wait_ge(setup.sem, 13)
            act.wait_ge(loaded_x.sem, 4 * 16)

            def squares(tiles):
                for t in tiles:
                    act.activation(HN[:, t, :], X[:, t, :], ACT.Square, accum_out=ss[:, t:t + 1])
                    act.drain()
                    act.activation(sd[:, t:t + 1], ss[:, t:t + 1], ACT.Sqrt, bias=eps_c[:, :], scale=1.0 / D_MODEL)\
                        .then_inc(sq_done.sem, 1)

            def turned(l, n, tiles):
                for t in tiles:
                    for a in range(TURNS):
                        act.wait_ge(*nt_ps.at(l, (n * TILES + t) * TURNS + a + 1))
                        act.activation(HT[:, a * KC // TURNS:(a + 1) * KC // TURNS, t * P:(t + 1) * P],
                                       bank(2 + a).rearrange("p (c k) -> p c k", k=P), ACT.Copy)\
                            .then_inc(nt_ev.sem, 1)

            def z_out(l, g, par, tiles):
                h = g * 2 + par
                for t in tiles:
                    if t == 0 and not (isinstance(g, int) and g == 0):
                        act.wait_ge(*att_done.at(l, g * 2 + (par - 1)))
                        act.wait_ge(*kv_stored.at(l, g * 2 + (par - 1)))
                    act.wait_ge(*z_ps.at(l, h * TILES + t + 1))
                    act.activation(ZH[par][:, t, :], bank((par * TILES + t) % 2, 0, 3 * HW), ACT.Copy)\
                        .then_inc(z_ev.sem, 1)

            def head(l, g, par, nxt):
                h = g * 2 + par
                act.wait_ge(*qt_ps.at(l, h + 1))
                for m in range(2):
                    d = slice(m * HD, (m + 1) * HD)
                    act.activation(QT[d, m, :], bank(2, 0, TOKD)[d], ACT.Copy).then_inc(qt_ev.sem, 1)
                if nxt is not None:
                    z_out(l, *nxt, [0])
                for t in range(TILES):
                    act.wait_ge(*nb_ready.at(l, h * TILES + t + 1))
                    n = P * (t + 1) if t < 2 else PAST + DEC_SEQ
                    for m in range(2):
                        src = (bank(4, m * n, (m + 1) * n), bank(6, m * n, (m + 1) * n),
                               bank(5 if m == 0 else 2, 0, n))[t]
                        act.activation(PR[t][:, m, :], src, ACT.Exp, bias=nb[:, t, m:m + 1], scale=SCALE,
                                       accum_out=sme[:, t, m:m + 1]).then_inc(ex_done.sem, 1)
                if nxt is not None:
                    z_out(l, *nxt, [1, 2])
                act.wait_ge(*pta_ps.at(l, h + 1))
                act.activation(PTA, bank(3, 0, 3 * P), ACT.Copy).then_inc(pta_ev.sem, 1)

            def exponents(l, n):
                act.wait_ge(*best_ready.at(l, n + 1))
                act.activation(GEX[:, :], BSM[:, :], ACT.Exp, accum_out=GSM[:, :]).then_inc(gex_ready.sem, 1)

            def weights(l, b, t):
                act.wait_ge(*av_ready.at(l, b + 1))
                act.activation(GV[:, :], AV[:, :], ACT.Gelu).then_inc(gv_ready.sem, 1)
                act.wait_ge(*wv_ready.at(l, b + 1))
                for s in range(BATCH):
                    act.wait_ge(*v_free.at(l, b * BATCH + (s + 1 - BATCH)))
                    act.activation(DG[:, s, :], (twins if t == 2 else ident)[:, :], ACT.Copy,
                                   scale=WV[:, s:s + 1]).then_inc(dg_ready.sem, 1)

            squares([0, 1])
            with act.Fori(0, DEPTH) as l:
                squares([2])
                turned(l, 0, range(TILES))

                def ff(u):
                    kind, j = FF_UNITS[u]
                    for k in range(2):
                        n, c = 2 * u + k, 2 * j + k
                        act.wait_ge(*ff_ps.at(l, n + 1))
                        src = bank(4 + n % 2, 0, TOK)
                        if kind == 1:
                            act.activation(YT[:, c, :], src, ACT.Gelu)
                        else:
                            buf, h0, s0 = ((XA, CONV_HIST, XA_S + CONV_HIST), None,
                                           (XQ, POOL_HIST, XQ_S + POOL_HIST))[kind]
                            act.activation(buf[:, c, h0:h0 + SEQ], src[:, 0:SEQ], ACT.Copy)
                            act.activation(buf[:, c, s0:s0 + DEC_SEQ], src[:, SEQ:TOK], ACT.Copy)
                        act.drain().then_inc(ff_ev.sem, 1)

                ff(0)
                act.wait_ge(*lam_dot.at(l, 1))
                act.activation(LE[:, :], LD[:, :], ACT.Exp).then_inc(lam_exp.sem, 1)
                act.wait_ge(*sp_in.at(l, 1))
                act.activation(spt[:, 1, :], spt[:, 0, :], ACT.Exp)
                act.drain()
                act.activation(spt[:, 2, :], spt[:, 1, :], ACT.Ln, bias=1.0).then_inc(sp_ln.sem, 1)
                for u in range(1, 5):
                    ff(u)
                act.wait_ge(*par_sb.at(l, 2))
                for c in range(RC):
                    for j, (dst, row) in enumerate(((RG, "lru_ba"), (IG, "lru_bx"))):
                        act.wait_ge(*bd_ps.at(l, 2 * c + j + 1))
                        act.activation(dst[:, c, :], bank(6 + j, 0, XC_W), ACT.Sigmoid,
                                       bias=PT[:, c, ROW[row]:ROW[row] + 1]).then_inc(sig_ev.sem, 1)
                act.wait_ge(*sp_out.at(l, 1))
                act.nop(nofuse=True)
                act.drain()
                for c in range(RC):
                    act.activation(DEC[:, c, :], RG[:, c, :], ACT.Exp, scale=nsp[:, c:c + 1])
                act.drain()
                for c in range(RC):
                    act.activation(RG[:, c, :], RG[:, c, :], ACT.Tanh, scale=nsp[:, c:c + 1])
                act.drain().then_inc(decay.sem, 1)
                ff(5)
                act.wait_ge(*oma.at(l, 1))
                act.activation(RG[:, :, :], RG[:, :, :], ACT.Sqrt).then_inc(root.sem, 1)
                z_out(l, 0, 0, range(TILES))
                for c in range(RC):
                    act.wait_ge(*pl_ps.at(l, c + 1))
                    act.activation(YT[:, RC + c, :], bank(4 + c % 2, 0, TOK), ACT.Copy,
                                   scale=PT[:, c, ROW["pool_scale"]:ROW["pool_scale"] + 1])\
                        .then_inc(pl_ev.sem, 1)
                with act.Fori(0, HEADS // 2 - 1) as g:
                    head(l, g, 0, (g, 1))
                    head(l, g, 1, (g + 1, 0))
                head(l, HEADS // 2 - 1, 0, (HEADS // 2 - 1, 1))
                head(l, HEADS // 2 - 1, 1, None)
                act.wait_ge(*sso_ready.at(l, 1))
                act.activation(rso[:, :, :], sso[:, :, :], ACT.Sqrt, bias=eps_c[:, :], scale=1.0 / HW)\
                    .then_inc(sso_root.sem, 1)
                def gates(dc, k):
                    act.wait_ge(*m_ev.at(l, dc - 1))
                    for b in range(N_BRANCH):
                        act.wait_ge(*gate_ps.at(l, dc * N_BRANCH + b + 1))
                        act.activation(SG[:, k, b, :], bank(b, 0, TOK), ACT.Sigmoid).then_inc(sg_ev.sem, 1)

                gates(0, 0)
                for hh in range(HEADS):
                    act.wait_ge(*yt_ps.at(l, hh + 1))
                    act.activation(YT[:, 2 * RC + hh, :], bank(6 + hh % 2, 0, TOK), ACT.Copy, scale=SUBG[:, 0:1])\
                        .then_inc(yt_ev.sem, 1)
                act.nop(nofuse=True)
                with act.Fori(0, GB - 1) as g:
                    gates(g * 2 + 1, 1)
                    gates(g * 2 + 2, 0)
                gates(2 * GB - 1, 1)
                def queries(n, k, tiles):
                    act.wait_ge(*pq_ps.at(l, n + (k + 1)))
                    act.activation(QS[:, k, 0:len(tiles) * P], bank(4 + k, 0, len(tiles) * P), ACT.Copy)\
                        .then_inc(pq_ev.sem, 1)

                def key_scores(n, row, tiles):
                    for k in range(2):
                        act.wait_ge(*sc_ps.at(l, n + (k + 1)))
                        to = SALL[:, tiles[0]:tiles[-1] + 1, bass.ds(row + k, 1), :]
                        act.activation(to.rearrange("p t a k -> p t (a k)"),
                                       bank(6 + k, 0, len(tiles) * P).rearrange("p (t k) -> p t k", t=len(tiles)),
                                       ACT.Copy).then_inc(sc_ev.sem, 1)

                for t in range(2):
                    act.wait_ge(*xo_ev.at(l, (t + 1) * GB))
                    squares([t])
                turned(l, 1, [0])
                for k in range(2):
                    queries(0, k, [0])
                key_scores(0, 0, [0])
                exponents(l, 0)
                act.wait_ge(*xo_ev.at(l, TILES * GB))
                squares([2])
                turned(l, 1, [1, 2])
                for n, row, tiles in ((2, 0, [1, 2]), (4, 2, range(TILES))):
                    for k in range(2):
                        queries(n, k, tiles)
                    key_scores(n, row, tiles)
                act.nop(nofuse=True)
                with act.Fori(0, PH - 2) as h:
                    weights(l, h * 2, 0)
                    exponents(l, h + 1)
                    queries(h * 2 + 6, 0, range(TILES))
                    weights(l, h * 2 + 1, 0)
                    queries(h * 2 + 6, 1, range(TILES))
                    key_scores(h * 2 + 6, h * 2 + 4, range(TILES))
                with act.Fori(PH - 2, PH) as h:
                    weights(l, h * 2, 0)
                    exponents(l, h + 1)
                    weights(l, h * 2 + 1, 0)

                def late_head(h, last):
                    b = h * 3 + FIRST_B
                    weights(l, b, 1)
                    exponents(l, h * 2 + (PH + 1))
                    weights(l, b + 1, 1)
                    if not last:
                        exponents(l, h * 2 + (PH + 2))
                    weights(l, b + 2, 2)

                with act.Fori(0, PH - 1) as h:
                    late_head(h, False)
                act.wait_ge(*x_done.at(l, 1))
                squares([0])
                late_head(PH - 1, True)
                act.wait_ge(*x_done.at(l, 2))
                squares([1])
                act.drain().then_inc(layer_done.sem, 1)
                act.wait_ge(*layer_done.at(l, 4))
            squares([2])

        @block.vector
        def _(dve):
            dve.wait_ge(setup.sem, 13)
            dve.wait_ge(loaded_x.sem, 4 * 16)

            def fence():
                dve.drain()

            def normed(l, n, t):
                dve.wait_ge(*sq_done.at(l, n * TILES + t + 1))
                dve.reciprocal(rstd[:, t:t + 1], sd[:, t:t + 1])
                fence()
                dve.wait_ge(*gain_in.at(l, n + 1))
                dve.scalar_tensor_tensor(out=HN[:, t, :], in0=X[:, t, :], scalar=rstd[:, t:t + 1],
                                         in1=G[:, :], op0=ALU.mult, op1=ALU.mult).then_inc(hn_ready.sem, 1)

            def head(l, g, par):
                h = g * 2 + par
                dve.wait_ge(*kt_ps.at(l, h + 1))
                dve.tensor_copy(KT[:, 0:SEQ], bank(3, 0, SEQ))
                dve.tensor_copy(KT[:, 2 * SEQ:2 * SEQ + P], bank(3, SEQ, SEQ + P))
                dve.tensor_copy(KT[:, SEQ:2 * SEQ], bank(5, 0, PAST))
                dve.drain().then_inc(kt_ev.sem, 1)
                for t in range(TILES):
                    dve.wait_ge(*s_ps.at(l, h * TILES + t + 1))
                    if t < 2:
                        n = P * (t + 1)
                        maps = bank(4 if t == 0 else 6, 0, 2 * n).rearrange("p (m k) -> p m k", m=2)
                        dve.memset(maps[0:CHUNK, :, n - CHUNK:n], FAR)
                        fence()
                        dve.tensor_reduce(mxs[:, t, :], maps, AX_X, ALU.max)
                    else:
                        for m in range(2):
                            dve.tensor_reduce(mxs[:, t, m:m + 1], bank(5 if m == 0 else 2, 0, PAST + DEC_SEQ),
                                              AX_X, ALU.max)
                    fence()
                    dve.tensor_scalar(nb[:, t, :], mxs[:, t, :], -SCALE, None, ALU.mult)\
                        .then_inc(nb_ready.sem, 1)
                for t in range(TILES):
                    n = P * (t + 1) if t < 2 else PAST + DEC_SEQ
                    dve.wait_ge(*ex_done.at(l, h * 2 * TILES + 2 * t + 2))
                    dve.reciprocal(rec[:, t, :], sme[:, t, :])
                    fence()
                    dve.tensor_tensor(rec[:, t, 1:2], rec[:, t, 1:2], neg_lam[:, :], ALU.mult)
                    dve.tensor_scalar(PC[t][:, 0:n], PR[t][:, 0, :], rec[:, t, 0:1], None, ALU.mult)
                    fence()
                    dve.scalar_tensor_tensor(out=PC[t][:, 0:n], in0=PR[t][:, 1, :], scalar=rec[:, t, 1:2],
                                             in1=PC[t][:, 0:n], op0=ALU.mult, op1=ALU.add)
                    dve.drain().then_inc(p_ready.sem, 1)
                dve.wait_ge(*ptb_ps.at(l, h + 1))
                dve.tensor_copy(PTB[:, :], bank(4, 0, 3 * P)).then_inc(ptb_ev.sem, 1)
                dve.wait_ge(*att_done.at(l, h + 1))
                dve.tensor_copy(OALL[:, :, h, :], bank(7, 0, 3 * P).rearrange("p (t e) -> p t e", t=TILES))\
                    .then_inc(o_ev.sem, 1)
                fence()
                o = OALL[:, :, bass.ds(h, 1), :].rearrange("p t a e -> p t (a e)")
                dve.tensor_tensor(SQ, o, o, ALU.mult)
                fence()
                dve.tensor_reduce(sso[:, :, bass.ds(h, 1)].rearrange("p t a -> p (t a)"), SQ, AX_X, ALU.add)

            def route(l, t, h):
                if t == 0:
                    dve.wait_ge(*sc_ev.at(l, 2 if isinstance(h, int) and h == 0 else h * 2 + 4))
                dve.tensor_copy(STG, SALL[:, t, bass.ds(h * 2, 2), :] if not isinstance(h, int)
                                else SALL[:, t, 2 * h:2 * h + 2, :])
                fence()
                for a in range(2):
                    dve.max(out=MX[:, a, 0:8], in_=STG[:, a, :])
                fence()
                for a in range(2):
                    dve.match_replace(out=STG2[:, a, :], in_to_replace=MX[:, a, 0:8], in_values=STG[:, a, :],
                                      imm_value=LOW)
                    dve.max_index(out=IX[:, a, 0:8], in_max=MX[:, a, 0:8], in_values=STG[:, a, :])
                fence()
                for a in range(2):
                    dve.max(out=MX[:, a, 8:16], in_=STG2[:, a, :])
                fence()
                for a in range(2):
                    dve.max_index(out=IX[:, a, 8:16], in_max=MX[:, a, 8:16], in_values=STG2[:, a, :])
                dve.tensor_tensor(CAND, MX[:, 0, :].unsqueeze(2).to_broadcast([P, TOPK, TOPK]),
                                  MX[:, 1, :].unsqueeze(1).to_broadcast([P, TOPK, TOPK]), ALU.add)
                fence()
                flat, flat2 = (x.rearrange("p a b -> p (a b)") for x in (CAND, CAND2))
                dve.max(out=BS[:, 0:8], in_=flat)
                dve.tensor_copy(IXF[:, :, :], IX[:, :, :])
                fence()
                dve.match_replace(out=flat2, in_to_replace=BS[:, 0:8], in_values=flat, imm_value=LOW)
                dve.max_index(out=BC[:, 0:8], in_max=BS[:, 0:8], in_values=flat)
                fence()
                dve.max(out=BS[:, 8:16], in_=flat2)
                fence()
                dve.max_index(out=BC[:, 8:16], in_max=BS[:, 8:16], in_values=flat2)
                dve.tensor_scalar(BSM[:, :], BS[:, :], BS[:, 0:1], None, ALU.subtract)\
                    .then_inc(best_ready.sem, 1)
                fence()
                dve.tensor_scalar(CI[:, 0, :], BC[:, :], 4, None, ALU.logical_shift_right)
                dve.tensor_scalar(CI[:, 1, :], BC[:, :], TOPK - 1, None, ALU.bitwise_and)
                fence()
                dve.tensor_copy(CIF[:, :, :], CI[:, :, :])
                fence()
                hot = [HOT[:, a, :].rearrange("p (k j) -> p k j", k=TOPK) for a in range(2)]
                for a in range(2):
                    dve.tensor_tensor(hot[a], CIF[:, a, :].unsqueeze(2).to_broadcast([P, TOPK, TOPK]),
                                      iota16[:, :].unsqueeze(1).to_broadcast([P, TOPK, TOPK]), ALU.is_equal)
                fence()
                for a in range(2):
                    dve.tensor_tensor(hot[a], hot[a], IXF[:, a, :].unsqueeze(1).to_broadcast([P, TOPK, TOPK]),
                                      ALU.mult)
                fence()
                for a in range(2):
                    dve.tensor_reduce(I12[:, a, :], hot[a], AX_X, ALU.add)
                fence()
                dve.scalar_tensor_tensor(out=IDF[:, :], in0=I12[:, 0, :], scalar=float(NK), in1=I12[:, 1, :],
                                         op0=ALU.mult, op1=ALU.add)
                fence()
                dve.tensor_scalar(IDX[:, :], IDF[:, :], LCON[:, 2:3], None, ALU.add)
                fence()

            def gates(l, n):
                dve.wait_ge(*gex_ready.at(l, n + 1))
                dve.reciprocal(GRC[:, :], GSM[:, :])
                fence()
                dve.tensor_scalar(GATE[:, :], GEX[:, :], GRC[:, :], None, ALU.mult)
                fence()

            def halves(t, k):
                if t < 2:
                    return [(slice(0, P), slice(k * BATCH, (k + 1) * BATCH))]
                return [(slice(i * CHUNK, (i + 1) * CHUNK), slice(i * BATCH, (i + 1) * BATCH)) for i in range(2)]

            def stage(l, b, i, t, k):
                dve.wait_ge(*v_free.at(l, (b - 1) * BATCH if not isinstance(b, int) or b >= 1 else 0))
                for r, c in halves(t, k):
                    dve.tensor_copy(STI[r, i, :], IDX[r, c])
                dve.drain().then_inc(idx_staged.sem, 1)

            def dots(l, b, t):
                for s in range(BATCH):
                    dve.wait_ge(*u_in[s].at(l, b + 1))
                    dve.tensor_tensor_reduce(RING_U[:, s, :], RING_U[:, s, :], HN[:, t, :], 1.0, 0.0,
                                             ALU.mult, ALU.add, AV[:, s:s + 1]).then_inc(u_free.sem, 1)
                dve.drain().then_inc(av_ready.sem, 1)

            def weigh(l, b, t, k):
                dve.wait_ge(*gv_ready.at(l, b + 1))
                for r, c in halves(t, k):
                    dve.tensor_tensor(WV[r, :], GV[r, :], GATE[r, c], ALU.mult)
                dve.drain().then_inc(wv_ready.sem, 1)

            def early_head(l, h, then):
                b = h * 2
                gates(l, h)
                dots(l, b, 0)
                stage(l, b + 1, 1, 0, 1)
                weigh(l, b, 0, 0)
                route(l, *then)
                dots(l, b + 1, 0)
                stage(l, b + 2, 0, then[0], 0)
                weigh(l, b + 1, 0, 1)

            def late_head(l, h, last):
                b = h * 3 + FIRST_B
                gates(l, h * 2 + PH)
                dots(l, b, 1)
                stage(l, b + 1, 1, 1, 1)
                weigh(l, b, 1, 0)
                route(l, 2, h)
                dots(l, b + 1, 1)
                stage(l, b + 2, 2, 2, 0)
                weigh(l, b + 1, 1, 1)
                gates(l, h * 2 + (PH + 1))
                if not last:
                    route(l, 1, h + 1)
                dots(l, b + 2, 2)
                if not last:
                    stage(l, b + 3, 0, 1, 0)
                weigh(l, b + 2, 2, 0)

            def clear(t):
                dve.memset(ps[:, D_MODEL * t:D_MODEL * (t + 1)], 0.0).then_inc(acc_clear.sem, 1)

            def add_experts(l, t, b):
                dve.wait_ge(*v_free.at(l, (b + 1) * BATCH))
                dve.tensor_tensor(X[:, t, :], X[:, t, :], ps[:, D_MODEL * t:D_MODEL * (t + 1)], ALU.add)

            with dve.Fori(0, DEPTH) as l:
                for t in range(TILES):
                    normed(l, 0, t)
                dve.drain().then_inc(gain_used.sem, 1)
                dve.wait_ge(*small_in.at(l, NSMALL))
                for a in range(2):
                    dve.tensor_tensor_reduce(LAMV[:, 2 * a, :], LAMV[:, 2 * a, :], LAMV[:, 2 * a + 1, :], 1.0, 0.0,
                                             ALU.mult, ALU.add, LD[:, a:a + 1])
                dve.tensor_tensor(SUBG[:, :], SUBG[:, :], LCON[:, 1:2], ALU.mult)
                dve.drain().then_inc(lam_dot.sem, 1)
                dve.wait_ge(*par_ps.at(l, 1))
                dve.tensor_copy(PT[:, :, :], bank(0).rearrange("p (c r) -> p c r", c=RC)[:, :, 0:NROW])\
                    .then_inc(par_sb.sem, 1)
                dve.wait_ge(*par_ps.at(l, 2))
                dve.tensor_copy(SKT[:, :, :], bank(1, 0, 2 * NK).rearrange("p (a k) -> p a k", a=2))\
                    .then_inc(par_sb.sem, 1)
                fence()
                L = PT[:, :, ROW["lru_L"]]
                dve.tensor_scalar(nsp[:, :], L, -1.0, 0.0, ALU.mult, ALU.max)
                dve.tensor_scalar(spt[:, 1, :], L, -1.0, None, ALU.mult)
                fence()
                dve.tensor_tensor(spt[:, 0, :], L, spt[:, 1, :], ALU.min)
                dve.drain().then_inc(sp_in.sem, 1)
                dve.wait_ge(*lam_exp.at(l, 1))
                dve.tensor_tensor(neg_lam[:, :], LE[:, 1:2], LE[:, 0:1], ALU.subtract)
                fence()
                dve.tensor_tensor(neg_lam[:, :], neg_lam[:, :], LCON[:, 0:1], ALU.subtract)
                dve.wait_ge(*sp_ln.at(l, 1))
                dve.tensor_tensor(nsp[:, :], nsp[:, :], spt[:, 2, :], ALU.add)
                fence()
                dve.tensor_scalar(nsp[:, :], nsp[:, :], -LRU_C, None, ALU.mult).then_inc(sp_out.sem, 1)
                dve.memset(XA[:, :, 0:CONV_HIST], 0.0)
                dve.memset(XQ[:, :, 0:POOL_HIST], 0.0)
                dve.tensor_copy(XA[:, :, XA_S:XA_S + CONV_HIST],
                                PT[:, :, ROW["conv_state"]:ROW["conv_state"] + CONV_HIST])
                dve.tensor_copy(XQ[:, :, XQ_S:XQ_S + POOL_HIST],
                                PT[:, :, ROW["pool_state"]:ROW["pool_state"] + POOL_HIST])
                dve.wait_ge(*ff_ev.at(l, 4))
                dve.nop(nofuse=True)
                fence()
                for j in range(CONV_W):
                    for c in range(RC):
                        w = PT[:, c, ROW["conv_w"] + j:ROW["conv_w"] + j + 1]
                        if j == 0:
                            dve.tensor_scalar(XC[:, c, :], XA[:, c, 0:XC_W], w,
                                              PT[:, c, ROW["conv_b"]:ROW["conv_b"] + 1], ALU.mult, ALU.add)
                        else:
                            dve.scalar_tensor_tensor(out=XC[:, c, :], in0=XA[:, c, j:j + XC_W], scalar=w,
                                                     in1=XC[:, c, :], op0=ALU.mult, op1=ALU.add)
                    fence()
                dve.drain().then_inc(xc_ready.sem, 1)
                dve.tensor_copy(SO[:, :, ST_CP:ST_CP + CONV_HIST], XA[:, :, SEQ:SEQ + CONV_HIST])
                dve.tensor_copy(SO[:, :, ST_CS:ST_CS + CONV_HIST], XA[:, :, XA_W - CONV_HIST:XA_W])
                dve.wait_ge(*ff_ev.at(l, 8))
                dve.tensor_tensor(S1[:, :, 1:XQ_W], XQ[:, :, 1:XQ_W], XQ[:, :, 0:XQ_W - 1], ALU.add)
                fence()
                dve.tensor_tensor(S2[:, 1:4, 3:XQ_W], S1[:, 1:4, 3:XQ_W], S1[:, 1:4, 1:XQ_W - 2], ALU.add)
                fence()
                dve.tensor_tensor(S1[:, 2:4, 7:XQ_W], S2[:, 2:4, 7:XQ_W], S2[:, 2:4, 3:XQ_W - 4], ALU.add)
                fence()
                dve.tensor_tensor(S2[:, 3, 15:XQ_W], S1[:, 3, 15:XQ_W], S1[:, 3, 7:XQ_W - 8], ALU.add)
                fence()
                dve.wait_ge(loaded_t.sem, 2 * 16)
                for c in range(RC):
                    for a, n, at in POOL_PARTS:
                        dve.tensor_tensor(SUMS[c][:, a:a + n], SUMS[c][:, a:a + n], PINV[:, c, at:at + n], ALU.mult)
                fence()
                for c in range(RC):
                    for a, n, at in POOL_PARTS:
                        dve.tensor_tensor(SUMS[c][:, a:a + n], SUMS[c][:, a:a + n], XQ[:, c, a:a + n], ALU.subtract)
                dve.drain().then_inc(d_ready.sem, 1)
                dve.wait_ge(*decay.at(l, 1))
                dve.tensor_scalar(XA[:, :, 0:XC_W], RG[:, :, :], -1.0, 1.0, ALU.mult, ALU.add)
                fence()
                dve.reciprocal(XA[:, :, 0:XC_W], XA[:, :, 0:XC_W])
                fence()
                dve.scalar_tensor_tensor(out=RG[:, :, :], in0=RG[:, :, :], scalar=-2.0, in1=XA[:, :, 0:XC_W],
                                         op0=ALU.mult, op1=ALU.mult)
                dve.drain().then_inc(oma.sem, 1)
                dve.tensor_tensor(IG[:, :, :], IG[:, :, :], XC[:, :, :], ALU.mult)
                dve.wait_ge(*root.at(l, 1))
                dve.nop(nofuse=True)
                fence()
                dve.tensor_tensor(IG[:, :, :], IG[:, :, :], RG[:, :, :], ALU.mult)
                fence()
                s0 = SEQ + CONV_HIST
                for c in range(RC):
                    dve.tensor_tensor_scan(RG[:, c, 0:SEQ], DEC[:, c, 0:SEQ], IG[:, c, 0:SEQ], 0.0,
                                           ALU.mult, ALU.add)
                    dve.tensor_tensor_scan(RG[:, c, s0:XC_W], DEC[:, c, s0:XC_W], IG[:, c, s0:XC_W],
                                           PT[:, c, ROW["lru_state"]:ROW["lru_state"] + 1],
                                           ALU.mult, ALU.add)
                fence()
                dve.wait_ge(*ff_ev.at(l, 12))
                dve.tensor_tensor(YT[:, 0:RC, 0:SEQ], YT[:, 0:RC, 0:SEQ], RG[:, :, 0:SEQ], ALU.mult)
                dve.tensor_tensor(YT[:, 0:RC, SEQ:TOK], YT[:, 0:RC, SEQ:TOK], RG[:, :, s0:XC_W], ALU.mult)
                dve.tensor_copy(SO[:, :, ST_PP:ST_PP + POOL_HIST], XQ[:, :, SEQ:SEQ + POOL_HIST])
                dve.tensor_copy(SO[:, :, ST_PS:ST_PS + POOL_HIST], XQ[:, :, XQ_W - POOL_HIST:XQ_W])
                dve.tensor_copy(SO[:, :, ST_LP:ST_LP + 1], RG[:, :, SEQ - 1:SEQ])
                dve.tensor_copy(SO[:, :, ST_LS:ST_LS + 1], RG[:, :, XC_W - 1:XC_W])
                dve.drain().then_inc(so_ready.sem, 1)
                dve.wait_ge(*so_ps.at(l, 1))
                dve.tensor_copy(SOT[:, :], bank(6)).then_inc(so_sb.sem, 1)

                dve.memset(PC[2][:, PAST + DEC_SEQ:3 * P], 0.0)
                dve.memset(QT[HD:P, 0, :], 0.0)
                dve.memset(QT[0:HD, 1, :], 0.0)
                with dve.Fori(0, HEADS // 2) as g:
                    for par in range(2):
                        head(l, g, par)
                fence()
                dve.drain().then_inc(sso_ready.sem, 1)
                dve.wait_ge(*sso_root.at(l, 1))
                dve.reciprocal(sso[:, :, :], rso[:, :, :])
                fence()
                for t in range(TILES):
                    dve.tensor_tensor(OALL[:, t], OALL[:, t],
                                      sso[:, t, :].unsqueeze(2).to_broadcast([P, HEADS, HW]), ALU.mult)
                dve.drain().then_inc(on_ready.sem, 1)
                with dve.Fori(0, GB) as g:
                    for k in range(2):
                        dc = g * 2 + k
                        m = MT[:, bass.ds(dc, 1), 0:TOK].rearrange("p a b -> p (a b)")
                        dve.wait_ge(*sg_ev.at(l, dc * N_BRANCH + N_BRANCH))
                        dve.wait_ge(*proj_ps.at(l, dc + 1))
                        for b in range(N_BRANCH):
                            dve.tensor_tensor(SG[:, k, b, :], SG[:, k, b, :], bank(3 + b, 0, TOK), ALU.mult)
                        fence()
                        dve.tensor_tensor(MTMP, SG[:, k, 0, :], SG[:, k, 1, :], ALU.add)
                        fence()
                        dve.tensor_tensor(m, MTMP, SG[:, k, 2, :], ALU.add).then_inc(m_ev.sem, 1)
                fence()
                dve.tensor_copy(MT[:, :, TOK:TOKD], MT[:, :, SEQ:TOK]).then_inc(mt_ready.sem, 1)

                def output(t):
                    for u in range(GB):
                        n = t * GB + u
                        dve.wait_ge(*xo_ps.at(l, n + 1))
                        x = X[:, t, u * UNIT:(u + 1) * UNIT]
                        dve.tensor_tensor(x, x, bank(xo_bank(n), 0, UNIT), ALU.add).then_inc(xo_ev.sem, 1)

                output(0)
                output(1)
                normed(l, 1, 0)
                normed(l, 1, 1)
                fence()
                route(l, 0, 0)
                output(2)
                stage(l, 0, 0, 0, 0)
                normed(l, 1, 2)
                clear(0)
                with dve.Fori(0, PH - 1) as h:
                    early_head(l, h, (0, h + 1))
                early_head(l, PH - 1, (1, 0))
                clear(1)
                dve.wait_ge(*sc_ev.at(l, Q_BLOCKS))
                clear(2)
                with dve.Fori(0, PH - 1) as h:
                    late_head(l, h, False)
                add_experts(l, 0, FIRST_B - 1)
                dve.drain().then_inc(x_done.sem, 1)
                late_head(l, PH - 1, True)
                add_experts(l, 1, BATCHES - 2)
                dve.drain().then_inc(x_done.sem, 1)
                add_experts(l, 2, BATCHES - 1)
                dve.drain().then_inc(layer_done.sem, 1)
                dve.wait_ge(*layer_done.at(l, 4))
            for t in range(TILES):
                normed(DEPTH, 0, t)
            dve.drain().then_inc(y_ready.sem, 1)


_INS = ['x_prompt', 'x_sample', 'cache_k', 'cache_v', 'state_conv', 'state_lru', 'state_pool',
        'norm1_g', 'w_in', 'conv_w', 'conv_b', 'lru_wa', 'lru_ba', 'lru_wx', 'lru_bx', 'lru_L',
        'pool_w', 'pool_scale', 'lam_q1', 'lam_k1', 'lam_q2', 'lam_k2', 'subln_g',
        'proj_a', 'proj_b', 'proj_c', 'w_out', 'norm2_g', 'peer_wq', 'peer_subkeys', 'peer_u', 'peer_v',
        'final_g']
_OUTS = [(1, 256, 1024), (1, 64, 1024),
         (2, 1, 256, 8, 2, 64), (2, 1, 256, 8, 128), (2, 1, 3, 512), (2, 1, 512), (2, 1, 15, 512),
         (2, 1, 64, 8, 2, 64), (2, 1, 64, 8, 128), (2, 1, 3, 512), (2, 1, 512), (2, 1, 15, 512)]


def constants():
    pos = np.concatenate([np.arange(SEQ), PAST + np.arange(DEC_SEQ), PAST + np.arange(DEC_SEQ)])
    inv = np.float32(500000.0) ** (-np.arange(ROT, dtype=np.float32) / np.float32(ROT))
    ang = pos.astype(np.float32)[:, None] * inv.astype(np.float32)[None, :]
    rot = np.stack([np.cos(ang), np.sin(ang)], axis=1).astype(np.float32).reshape(TILES, P, 2, ROT)
    t = np.concatenate([np.arange(SEQ), PAST + np.arange(DEC_SEQ)])
    counts = np.stack([np.minimum(t + 1, w) for w in (2, 4, 8, 16)])
    pool_inv = (1.0 / counts).astype(np.float32)
    lam = [0.8 - 0.6 * np.exp(-0.3 * l) for l in range(DEPTH)]
    lc = np.array([[x, 1.0 - x, l * N_EXPERTS] for l, x in enumerate(lam)], np.float32)
    return {"rot_table": rot, "pool_inv": pool_inv, "layer_consts": lc}


def kernel(**inputs):
    import numpy as _np
    import concourse.bacc as _bacc
    from concourse import mybir as _mybir
    from concourse.bass_utils import run_bass_kernel_spmd as _run

    nc = _bacc.Bacc("TRN2", target_bir_lowering=False, num_devices=1)
    arrays, args = {}, []
    for name, a in [(n, inputs[n]) for n in _INS] + list(constants().items()):
        a = _np.ascontiguousarray(a)
        arrays[f"in_{name}_dram"] = a
        args.append(nc.dram_tensor(f"in_{name}_dram", a.shape, _mybir.dt.from_np(a.dtype), kind="ExternalInput").ap())
    for i, shape in enumerate(_OUTS):
        args.append(nc.dram_tensor(f"out_{i}_dram", shape, _mybir.dt.float32, kind="ExternalOutput").ap())
    build(nc, *args)
    r = _run(nc, [arrays], core_ids=[0])
    return tuple(r.results[0][f"out_{i}_dram"] for i in range(len(_OUTS)))
```
